# Optimizing a Trainium2 kernel written in Bass

```python
import math
import jax, jax.numpy as jnp
from jax import lax
import numpy as np

D_MODEL = 1024
BATCH = 1
SEQ = 256
DEPTH = 1

PLE_DIM = 256
SGU_CHUNK = 128
SGU_GROUPS = 8
SGU_WIDTH = D_MODEL
SGU_GROUP_DIM = SGU_WIDTH // SGU_GROUPS
ATT_HEADS = 16
HEAD_DIM = 64
ATT_WIDTH = ATT_HEADS * HEAD_DIM
MOBA_BLOCK = 256
MOBA_TOPK = 3
Q_CHUNK = 64
REL_BUCKETS = 32
REL_MAX_DIST = 1024
D_FF = 4 * D_MODEL
EPS = 1e-6
SPLITS = (SGU_WIDTH, SGU_WIDTH, ATT_WIDTH, ATT_WIDTH, ATT_WIDTH, D_MODEL, D_MODEL)
IN_COLS = sum(SPLITS)


def rms_norm(x, g):
    xf = x.astype(jnp.float32)
    y = xf * lax.rsqrt(jnp.mean(xf * xf, axis=-1, keepdims=True) + EPS)
    return (y * g.astype(jnp.float32)).astype(x.dtype)

def layer_norm(x, g, b):
    xf = x.astype(jnp.float32)
    mu = jnp.mean(xf, axis=-1, keepdims=True)
    xc = xf - mu
    y = xc * lax.rsqrt(jnp.mean(xc * xc, axis=-1, keepdims=True) + EPS)
    return (y * g.astype(jnp.float32) + b.astype(jnp.float32)).astype(x.dtype)

def rel_bucket(dist):
    n = jnp.maximum(dist, 0)
    max_exact = REL_BUCKETS // 2
    nf = jnp.maximum(n, max_exact).astype(jnp.float32)
    large = max_exact + (jnp.log(nf / max_exact) / math.log(REL_MAX_DIST / max_exact)
                         * (REL_BUCKETS - max_exact)).astype(jnp.int32)
    large = jnp.minimum(large, REL_BUCKETS - 1)
    return jnp.where(n < max_exact, n, large)

def sgu_mixer(u, v, w_s, b_s, ln_g, ln_b):
    B, S, _ = u.shape
    nc = S // SGU_CHUNK
    v = layer_norm(v, ln_g, ln_b)
    vg = v.reshape(B, nc, SGU_CHUNK, SGU_GROUPS, SGU_GROUP_DIM)
    causal = jnp.tril(jnp.ones((SGU_CHUNK, SGU_CHUNK), dtype=bool))
    w = jnp.where(causal, w_s, 0).astype(v.dtype)
    mixed = jnp.einsum('gts,bnsgc->bntgc', w, vg) + b_s.T[None, None, :, :, None].astype(v.dtype)
    return u * mixed.reshape(B, S, SGU_WIDTH)

_gather_blocks = jax.vmap(jax.vmap(lambda blocks, idx: blocks[idx]))

def moba_attention(q, k, v, rel_bias):
    B, H, S, dh = q.shape
    nb = S // MOBA_BLOCK
    topk = min(MOBA_TOPK, nb)
    kb = k.reshape(B, H, nb, MOBA_BLOCK, dh)
    vb = v.reshape(B, H, nb, MOBA_BLOCK, dh)
    k_mean = jnp.mean(kb.astype(jnp.float32), axis=3).astype(k.dtype)
    scale = dh ** -0.5
    table = rel_bias.T
    h_idx = jnp.arange(H)[None, :, None, None, None]
    pos_in_block = jnp.arange(MOBA_BLOCK)
    n_chunks = S // Q_CHUNK
    q_chunks = q.reshape(B, H, n_chunks, Q_CHUNK, dh).transpose(2, 0, 1, 3, 4)
    n_sel = topk * MOBA_BLOCK

    def one_chunk(args):
        c, q_c = args
        q_pos = c * Q_CHUNK + jnp.arange(Q_CHUNK)
        own = (c * Q_CHUNK) // MOBA_BLOCK
        gate = jnp.einsum('bhqd,bhnd->bhqn', q_c, k_mean).astype(jnp.float32)
        gate = jnp.where(jnp.arange(nb) < own, gate, -jnp.inf)
        _, sel = lax.top_k(gate, topk)
        sel_valid = sel < own
        k_sel = _gather_blocks(kb, sel)
        v_sel = _gather_blocks(vb, sel)
        s_sel = jnp.einsum('bhqd,bhqkmd->bhqkm', q_c, k_sel).astype(jnp.float32) * scale
        k_pos_sel = sel[..., None] * MOBA_BLOCK + pos_in_block
        dist_sel = q_pos[:, None, None] - k_pos_sel
        s_sel = s_sel + table[h_idx, rel_bucket(dist_sel)].astype(jnp.float32)
        s_sel = jnp.where(sel_valid[..., None], s_sel, -jnp.inf)
        k_own = lax.dynamic_index_in_dim(kb, own, axis=2, keepdims=False)
        v_own = lax.dynamic_index_in_dim(vb, own, axis=2, keepdims=False)
        s_own = jnp.einsum('bhqd,bhmd->bhqm', q_c, k_own).astype(jnp.float32) * scale
        dist_own = q_pos[:, None] - (own * MOBA_BLOCK + pos_in_block)[None, :]
        s_own = s_own + table[:, rel_bucket(dist_own)].astype(jnp.float32)
        s_own = jnp.where(dist_own >= 0, s_own, -jnp.inf)
        s_all = jnp.concatenate([s_sel.reshape(B, H, Q_CHUNK, n_sel), s_own], axis=-1)
        probs = jax.nn.softmax(s_all, axis=-1).astype(v.dtype)
        p_sel = probs[..., :n_sel].reshape(B, H, Q_CHUNK, topk, MOBA_BLOCK)
        p_own = probs[..., n_sel:]
        return (jnp.einsum('bhqkm,bhqkmd->bhqd', p_sel, v_sel)
                + jnp.einsum('bhqm,bhmd->bhqd', p_own, v_own))

    out = lax.map(one_chunk, (jnp.arange(n_chunks), q_chunks))
    return out.transpose(1, 2, 0, 3, 4).reshape(B, H, S, dh)

def first_inputs(seed: int = 0) -> dict:
    key = jax.random.key(seed)
    ks = jax.random.split(key, 20)
    f32 = jnp.float32
    nrm = lambda k, shape, s: jax.random.normal(k, shape, f32) * s
    L = DEPTH
    return {
        "x": nrm(ks[0], (BATCH, SEQ, D_MODEL), 1.0),
        "p": nrm(ks[1], (DEPTH, BATCH, SEQ, PLE_DIM), 1.0),
        "norm_mix_g": 1.0 + nrm(ks[2], (L, D_MODEL), 0.05),
        "w_in": nrm(ks[3], (L, D_MODEL, IN_COLS), D_MODEL ** -0.5),
        "w_sgu_spatial": nrm(ks[4], (L, SGU_GROUPS, SGU_CHUNK, SGU_CHUNK), SGU_CHUNK ** -0.5),
        "b_sgu_spatial": 1.0 + nrm(ks[5], (L, SGU_GROUPS, SGU_CHUNK), 0.1),
        "ln_v_g": 1.0 + nrm(ks[6], (L, SGU_WIDTH), 0.05),
        "ln_v_b": nrm(ks[7], (L, SGU_WIDTH), 0.02),
        "rel_bias": nrm(ks[8], (REL_BUCKETS, ATT_HEADS), 0.5),
        "w_out": nrm(ks[9], (L, D_MODEL, D_MODEL), D_MODEL ** -0.5),
        "norm_ffn_g": 1.0 + nrm(ks[10], (L, D_MODEL), 0.05),
        "w_ff1": nrm(ks[11], (L, D_MODEL, D_FF), D_MODEL ** -0.5),
        "w_ff2": nrm(ks[12], (L, D_FF, D_MODEL), D_FF ** -0.5),
        "norm_ple_g": 1.0 + nrm(ks[13], (L, D_MODEL), 0.05),
        "w_ple_gate": nrm(ks[14], (L, D_MODEL, D_MODEL), D_MODEL ** -0.5),
        "w_ple_proj": nrm(ks[15], (L, PLE_DIM, D_MODEL), PLE_DIM ** -0.5),
        "norm_final_g": 1.0 + nrm(ks[16], (D_MODEL,), 0.05),
    }

def first_block(x, p, norm_mix_g, w_in, w_sgu_spatial, b_sgu_spatial, ln_v_g, ln_v_b, rel_bias,
              w_out, norm_ffn_g, w_ff1, w_ff2, norm_ple_g, w_ple_gate, w_ple_proj, norm_final_g):
    B, S, _ = x.shape
    offsets = np.cumsum(SPLITS)[:-1].tolist()
    for i in range(DEPTH):
        h = rms_norm(x, norm_mix_g[i])
        proj = h @ w_in[i]
        za_u, za_v, q, k, v_att, g_a, g_b = jnp.split(proj, offsets, axis=-1)
        y_a = sgu_mixer(jax.nn.gelu(za_u), jax.nn.gelu(za_v), w_sgu_spatial[i], b_sgu_spatial[i],
                        ln_v_g[i], ln_v_b[i])
        heads = lambda t: t.reshape(B, S, ATT_HEADS, HEAD_DIM).transpose(0, 2, 1, 3)
        y_b = moba_attention(heads(q), heads(k), heads(v_att), rel_bias)
        y_b = y_b.transpose(0, 2, 1, 3).reshape(B, S, ATT_WIDTH)
        merged = jax.nn.sigmoid(g_a) * y_a + jax.nn.sigmoid(g_b) * y_b
        x = x + merged @ w_out[i]
        h = rms_norm(x, norm_ffn_g[i])
        x = x + jnp.square(jax.nn.relu(h @ w_ff1[i])) @ w_ff2[i]
        gate = jax.nn.sigmoid(rms_norm(x, norm_ple_g[i]) @ w_ple_gate[i])
        x = x + gate * (p[i] @ w_ple_proj[i])
    return rms_norm(x, norm_final_g)


SSD_HEAD_DIM = 64
D_SSD = D_MODEL
SSD_HEADS = D_SSD // SSD_HEAD_DIM
SSD_GROUPS = 2
SSD_STATE = 128
CONV_K = 4
SSD_CHUNK = 128
CONV_CH = D_SSD + 2 * SSD_GROUPS * SSD_STATE
ATTN_HEAD_DIM = 64
D_ATTN = D_MODEL
ATTN_Q_HEADS = D_ATTN // ATTN_HEAD_DIM
ATTN_KV_HEADS = 2
Q_PER_KV = ATTN_Q_HEADS // ATTN_KV_HEADS
D_KV = ATTN_KV_HEADS * ATTN_HEAD_DIM
WINDOW = 128
ATTN_SCALE = ATTN_HEAD_DIM ** -0.5
D_MIX = D_SSD + D_ATTN
SPLITS_2 = (D_SSD,
          D_SSD + CONV_CH,
          D_SSD + CONV_CH + SSD_HEADS,
          D_SSD + CONV_CH + SSD_HEADS + D_ATTN,
          D_SSD + CONV_CH + SSD_HEADS + D_ATTN + D_KV)
IN_DIM = D_SSD + CONV_CH + SSD_HEADS + D_ATTN + 2 * D_KV
MOE_GROUPS = 8
EXPERTS_PER_GROUP = 8
N_EXPERTS = MOE_GROUPS * EXPERTS_PER_GROUP
TOP_K = 2
D_FF_EXPERT = D_MODEL // 2
MOE_BLOCK = 128


def rmsnorm(x, g):
    xf = x.astype(jnp.float32)
    y = xf * lax.rsqrt(jnp.mean(xf * xf, axis=-1, keepdims=True) + EPS)
    return (y * g.astype(jnp.float32)).astype(x.dtype)

def causal_depthwise_conv(u, w, b):
    c = u.shape[-1]
    y = lax.conv_general_dilated(u, w[:, None, :], window_strides=(1,),
                                 padding=[(CONV_K - 1, 0)],
                                 dimension_numbers=("NWC", "WIO", "NWC"),
                                 feature_group_count=c)
    return y + b

def ssd_chunked(x, dt, A, B, C):
    b, s, h, p = x.shape
    g, n = B.shape[2], B.shape[3]
    r = h // g
    c = s // SSD_CHUNK
    L = SSD_CHUNK
    xc = x.reshape(b, c, L, g, r, p)
    dtc = dt.reshape(b, c, L, g, r)
    Bc = B.reshape(b, c, L, g, n)
    Cc = C.reshape(b, c, L, g, n)
    a = jnp.moveaxis(dtc * A.reshape(g, r), 2, -1)
    a_cs = jnp.cumsum(a, axis=-1)
    xdt = xc * dtc[..., None]
    idx = jnp.arange(L)
    causal = idx[:, None] >= idx[None, :]
    seg = a_cs[..., :, None] - a_cs[..., None, :]
    decay = jnp.exp(jnp.where(causal, seg, -jnp.inf))
    cb = jnp.einsum("bclgn,bcsgn->bcgls", Cc, Bc)
    y_diag = jnp.einsum("bcgls,bcgrls,bcsgrp->bclgrp", cb, decay, xdt)
    decay_to_end = jnp.exp(a_cs[..., -1:] - a_cs)
    states = jnp.einsum("bclgn,bcgrl,bclgrp->bcgrpn", Bc, decay_to_end, xdt)
    chunk_decay = jnp.exp(a_cs[..., -1])

    def step(carry, inp):
        st, dec = inp
        return carry * dec[..., None, None] + st, carry

    init = jnp.zeros((b, g, r, p, n), states.dtype)
    _, prev = lax.scan(step, init, (jnp.moveaxis(states, 1, 0), jnp.moveaxis(chunk_decay, 1, 0)))
    prev = jnp.moveaxis(prev, 0, 1)
    y_off = jnp.einsum("bclgn,bcgrpn,bcgrl->bclgrp", Cc, prev, jnp.exp(a_cs))
    return (y_diag + y_off).reshape(b, s, h, p)

def gated_group_rmsnorm(y, z, gain):
    u = y * jax.nn.silu(z.astype(jnp.float32))
    u = u.reshape(*y.shape[:-1], SSD_GROUPS, -1)
    u = u * lax.rsqrt(jnp.mean(u * u, axis=-1, keepdims=True) + EPS)
    return u.reshape(y.shape) * gain.astype(jnp.float32)

def swa_gqa_sinks(q, k, v, sinks):
    b, s = q.shape[0], q.shape[1]
    nb = s // WINDOW
    W = WINDOW
    qb = q.astype(jnp.float32).reshape(b, nb, W, ATTN_KV_HEADS, Q_PER_KV, ATTN_HEAD_DIM) * ATTN_SCALE
    kb = k.astype(jnp.float32).reshape(b, nb, W, ATTN_KV_HEADS, ATTN_HEAD_DIM)
    vb = v.astype(jnp.float32).reshape(b, nb, W, ATTN_KV_HEADS, ATTN_HEAD_DIM)
    pad = ((0, 0), (1, 0), (0, 0), (0, 0), (0, 0))
    kcat = jnp.concatenate([jnp.pad(kb, pad)[:, :-1], kb], axis=2)
    vcat = jnp.concatenate([jnp.pad(vb, pad)[:, :-1], vb], axis=2)
    scores = jnp.einsum("bnqhrd,bnkhd->bnhrqk", qb, kcat)
    qi = jnp.arange(W)[:, None]
    kj = jnp.arange(2 * W)[None, :]
    rel = qi + W - kj
    band = (rel >= 0) & (rel < WINDOW)
    blk = jnp.arange(nb)[:, None, None]
    valid = band[None] & ((blk > 0) | (kj >= W)[None])
    scores = jnp.where(valid[None, :, None, None], scores, -jnp.inf)
    sink = sinks.astype(jnp.float32).reshape(ATTN_KV_HEADS, Q_PER_KV)[None, None, :, :, None, None]
    m = jnp.maximum(jnp.max(scores, axis=-1, keepdims=True), sink)
    pr = jnp.exp(scores - m)
    denom = jnp.sum(pr, axis=-1, keepdims=True) + jnp.exp(sink - m)
    out = jnp.einsum("bnhrqk,bnkhd->bnqhrd", pr / denom, vcat)
    return out.reshape(b, s, ATTN_Q_HEADS * ATTN_HEAD_DIM)

def hybrid_mixer(h, w_in, conv_w, conv_b, dt_bias, a_log, d_skip, ssd_norm,
                 attn_sinks, attn_norm, w_out):
    b, s, _ = h.shape
    proj = h @ w_in
    z, xbc, dt_raw, q, k, v = jnp.split(proj, SPLITS_2, axis=-1)
    xbc = jax.nn.silu(causal_depthwise_conv(xbc, conv_w, conv_b)).astype(jnp.float32)
    xs, Bm, Cm = jnp.split(xbc, (D_SSD, D_SSD + SSD_GROUPS * SSD_STATE), axis=-1)
    xs = xs.reshape(b, s, SSD_HEADS, SSD_HEAD_DIM)
    dt = jax.nn.softplus(dt_raw.astype(jnp.float32) + dt_bias.astype(jnp.float32))
    A = -jnp.exp(a_log.astype(jnp.float32))
    y = ssd_chunked(xs, dt, A,
                    Bm.reshape(b, s, SSD_GROUPS, SSD_STATE),
                    Cm.reshape(b, s, SSD_GROUPS, SSD_STATE))
    y = y + xs * d_skip.astype(jnp.float32)[:, None]
    y_ssd = gated_group_rmsnorm(y.reshape(b, s, D_SSD), z, ssd_norm)
    att = swa_gqa_sinks(q.reshape(b, s, ATTN_Q_HEADS, ATTN_HEAD_DIM),
                        k.reshape(b, s, ATTN_KV_HEADS, ATTN_HEAD_DIM),
                        v.reshape(b, s, ATTN_KV_HEADS, ATTN_HEAD_DIM), attn_sinks)
    y_att = rmsnorm(att, attn_norm)
    mixed = jnp.concatenate([y_ssd, y_att], axis=-1).astype(h.dtype)
    return mixed @ w_out

def hierarchical_moe(h, w_router_group, w_router_expert, w_gate, w_up, w_down):
    b, s, d = h.shape
    t = h.reshape(-1, d)
    n = t.shape[0]
    rows = jnp.arange(n)
    group_logits = (t @ w_router_group).astype(jnp.float32)
    group_prob = jax.nn.softmax(group_logits, axis=-1)
    g_sel = jnp.argmax(group_logits, axis=-1)
    p_group = group_prob[rows, g_sel][:, None]
    exp_logits = (t @ w_router_expert).astype(jnp.float32).reshape(n, MOE_GROUPS, EXPERTS_PER_GROUP)
    in_group = exp_logits[rows, g_sel]
    top_logit, top_local = lax.top_k(in_group, TOP_K)
    gate = jax.nn.softmax(top_logit, axis=-1) * p_group
    expert_id = g_sel[:, None] * EXPERTS_PER_GROUP + top_local
    a = n * TOP_K
    flat_e = expert_id.reshape(-1)
    flat_g = gate.reshape(-1)
    order = jnp.argsort(flat_e)
    e_sorted = flat_e[order]
    tok_sorted = order // TOP_K
    counts = jnp.bincount(flat_e, length=N_EXPERTS)
    padded = ((counts + MOE_BLOCK - 1) // MOE_BLOCK) * MOE_BLOCK
    start = jnp.cumsum(counts) - counts
    pend = jnp.cumsum(padded)
    pstart = pend - padded
    dest = pstart[e_sorted] + jnp.arange(a) - start[e_sorted]
    n_blocks = -(-(a + N_EXPERTS * (MOE_BLOCK - 1)) // MOE_BLOCK)
    buf = jnp.zeros((n_blocks * MOE_BLOCK, d), t.dtype).at[dest].set(t[tok_sorted])
    block_expert = jnp.minimum(
        jnp.searchsorted(pend, jnp.arange(n_blocks) * MOE_BLOCK, side="right"), N_EXPERTS - 1)

    def expert_block(args):
        xb, e = args
        hid = jax.nn.silu(xb @ w_gate[e]) * (xb @ w_up[e])
        return hid @ w_down[e]

    y_buf = lax.map(expert_block, (buf.reshape(n_blocks, MOE_BLOCK, d), block_expert))
    y_buf = y_buf.reshape(-1, d)
    y = jnp.zeros_like(t).at[tok_sorted].add(y_buf[dest] * flat_g[order][:, None].astype(t.dtype))
    return y.reshape(b, s, d)

def second_inputs(seed: int = 0) -> dict:
    key = jax.random.key(seed)
    ks = jax.random.split(key, 20)
    f32 = jnp.float32
    nrm = lambda k, shp, sc: jax.random.normal(k, shp, f32) * sc
    dt0 = jnp.exp(jax.random.uniform(ks[5], (DEPTH, SSD_HEADS), f32)
                  * (math.log(0.1) - math.log(1e-3)) + math.log(1e-3))
    return {
        "x": nrm(ks[0], (BATCH, SEQ, D_MODEL), 1.0),
        "norm_mix": 1.0 + nrm(ks[1], (DEPTH, D_MODEL), 0.02),
        "w_in": nrm(ks[2], (DEPTH, D_MODEL, IN_DIM), D_MODEL ** -0.5),
        "conv_w": nrm(ks[3], (DEPTH, CONV_K, CONV_CH), CONV_K ** -0.5),
        "conv_b": nrm(ks[4], (DEPTH, CONV_CH), 0.02),
        "dt_bias": dt0 + jnp.log(-jnp.expm1(-dt0)),
        "a_log": jnp.log(jax.random.uniform(ks[6], (DEPTH, SSD_HEADS), f32, 1.0, 16.0)),
        "d_skip": 1.0 + nrm(ks[7], (DEPTH, SSD_HEADS), 0.02),
        "ssd_norm": 1.0 + nrm(ks[8], (DEPTH, D_SSD), 0.02),
        "attn_sinks": nrm(ks[9], (DEPTH, ATTN_Q_HEADS), 0.5),
        "attn_norm": 1.0 + nrm(ks[10], (DEPTH, D_ATTN), 0.02),
        "w_out": nrm(ks[11], (DEPTH, D_MIX, D_MODEL), D_MIX ** -0.5),
        "norm_ffn": 1.0 + nrm(ks[12], (DEPTH, D_MODEL), 0.02),
        "w_router_group": nrm(ks[13], (DEPTH, D_MODEL, MOE_GROUPS), D_MODEL ** -0.5),
        "w_router_expert": nrm(ks[14], (DEPTH, D_MODEL, N_EXPERTS), D_MODEL ** -0.5),
        "w_gate": nrm(ks[15], (DEPTH, N_EXPERTS, D_MODEL, D_FF_EXPERT), D_MODEL ** -0.5),
        "w_up": nrm(ks[16], (DEPTH, N_EXPERTS, D_MODEL, D_FF_EXPERT), D_MODEL ** -0.5),
        "w_down": nrm(ks[17], (DEPTH, N_EXPERTS, D_FF_EXPERT, D_MODEL), D_FF_EXPERT ** -0.5),
        "norm_final": 1.0 + nrm(ks[18], (D_MODEL,), 0.02),
    }

def second_block(x, norm_mix, w_in, conv_w, conv_b, dt_bias, a_log, d_skip, ssd_norm,
              attn_sinks, attn_norm, w_out, norm_ffn, w_router_group, w_router_expert,
              w_gate, w_up, w_down, norm_final):
    h = x
    for l in range(DEPTH):
        h = h + hybrid_mixer(rmsnorm(h, norm_mix[l]), w_in[l], conv_w[l], conv_b[l],
                             dt_bias[l], a_log[l], d_skip[l], ssd_norm[l],
                             attn_sinks[l], attn_norm[l], w_out[l])
        h = h + hierarchical_moe(rmsnorm(h, norm_ffn[l]), w_router_group[l],
                                 w_router_expert[l], w_gate[l], w_up[l], w_down[l])
    return rmsnorm(h, norm_final)


def setup_inputs(seed=0):
    out = dict(first_inputs(seed))
    for name, value in second_inputs(seed + 1).items():
        if name != "x":
            out[name + "_2"] = value
    return out


def reference(
    x, p, norm_mix_g, w_in, w_sgu_spatial, b_sgu_spatial, ln_v_g, ln_v_b, rel_bias, w_out,
    norm_ffn_g, w_ff1, w_ff2, norm_ple_g, w_ple_gate, w_ple_proj, norm_final_g, norm_mix_2,
    w_in_2, conv_w_2, conv_b_2, dt_bias_2, a_log_2, d_skip_2, ssd_norm_2, attn_sinks_2,
    attn_norm_2, w_out_2, norm_ffn_2, w_router_group_2, w_router_expert_2, w_gate_2, w_up_2,
    w_down_2, norm_final_2,
):
    x = first_block(
        x, p, norm_mix_g, w_in, w_sgu_spatial, b_sgu_spatial, ln_v_g, ln_v_b, rel_bias, w_out,
        norm_ffn_g, w_ff1, w_ff2, norm_ple_g, w_ple_gate, w_ple_proj, norm_final_g,
    )
    return second_block(
        x, norm_mix_2, w_in_2, conv_w_2, conv_b_2, dt_bias_2, a_log_2, d_skip_2, ssd_norm_2,
        attn_sinks_2, attn_norm_2, w_out_2, norm_ffn_2, w_router_group_2, w_router_expert_2,
        w_gate_2, w_up_2, w_down_2, norm_final_2,
    )


_drawn_inputs = setup_inputs


def setup_inputs(seed=0):
    import zlib

    import numpy as np

    out = dict(_drawn_inputs(seed))
    spreads = {}
    factors = {'ln_v_g': 3.988,
     'ln_v_b': 6.666,
     'norm_ple_g': 5.083,
     'conv_b_2': 2.727,
     'd_skip_2': 6.491,
     'ssd_norm_2': 3.778,
     'attn_sinks_2': 5.111,
     'attn_norm_2': 2.793,
     'norm_ffn_2': 4.178,
     'norm_final_2': 2.818}
    for name, (base, spread) in spreads.items():
        noise = np.random.default_rng([zlib.crc32(name.encode()), seed]).standard_normal(out[name].shape)
        drawn = base * np.exp(spread * noise) if base else spread * noise
        out[name] = __import__('jax').numpy.asarray(drawn.astype(out[name].dtype))
    for name, factor in factors.items():
        out[name] = (out[name] * factor).astype(out[name].dtype)
    return out
```

```python
from contextlib import ExitStack

import numpy as np

import concourse.bass as bass
from concourse import mybir

F32 = mybir.dt.float32
I32 = mybir.dt.int32
ALU = mybir.AluOpType
ACT = mybir.ActivationFunctionType
AX_X = mybir.AxisListType.X

P = 128
D = 1024
S = 256
MT = S // P
KT = D // P
HEADS, DH = 16, 64
GROUPS = 8
BUCKETS = 32
D_FF = 4096
FT = D_FF // P
LINE = 512
SSD_G, SSD_N = 2, 128
CT = 12
TAPS = 4
NE, EG = 64, 8
FE = 512
SLOTS = 64
PAIRS = NE // 2
PASSES = S // SLOTS
EPS = 1e-6
MASKED = -1e30
RING = 6
Q_SCALE = DH ** -0.5

PANELS = ([("v", 0), ("v", 1), ("u", 0), ("u", 1), ("q", 0), ("q", 1), ("k", 0), ("k", 1),
           ("va", 0), ("va", 1), ("gb", 0), ("gb", 1), ("ga", 0), ("ga", 1), ("wo", 0), ("wo", 1)]
          + [("ff1", j) for j in range(8)] + [("ff2", j) for j in range(8)]
          + [("pp", 0), ("pg", 0), ("pg", 1)]
          + [("q2", 0), ("q2", 1), ("kv2", 0), ("xbc", 0), ("xbc", 1), ("xbc", 2), ("z", 0), ("z", 1)]
          + [("wo2", 2), ("wo2", 3), ("wo2", 0), ("wo2", 1)])
NP = len(PANELS)
AT = {panel: p for p, panel in enumerate(PANELS)}
EMPTIED_BY = {"v": "aa", "u": "aa", "q": "ad", "k": "ad", "va": "ad", "gb": "aa", "ga": "aa", "wo": "dd",
              "ff1": "aa", "ff2": "", "pp": "", "pg": "aa", "q2": "ad", "kv2": "ad", "xbc": "ad",
              "z": "aa", "wo2": ""}
ROWS = {}
for _name, _n in (("norm_mix_g", 8), ("norm_ffn_g", 8), ("norm_ple_g", 8), ("b_sgu", 8), ("norm_mix_2", 8),
                  ("conv_w", TAPS * CT), ("conv_b", CT), ("ssd_norm", 8), ("attn_norm", 8), ("norm_ffn_2", 8)):
    ROWS[_name] = (sum(n for _, n in ROWS.values()), _n)
NROWS = sum(n for _, n in ROWS.values())


def emptied(engine, p):
    return sum(EMPTIED_BY[kind].count(engine) for kind, _ in PANELS[:p + 1])


def pair_of(p):
    return 2 * (sum(1 for kind, _ in PANELS[:p] if EMPTIED_BY[kind]) % 2)


def before_in_pair(p):
    users = [q for q in range(p) if EMPTIED_BY[PANELS[q][0]] and pair_of(q) == pair_of(p)]
    return users[-1] if users else None


def program(nc, x_in, p_in, norm_mix_g, w_in, w_sgu, b_sgu, ln_v_g, ln_v_b, rel_bias, w_out, norm_ffn_g,
            w_ff1, w_ff2, norm_ple_g, w_ple_gate, w_ple_proj, norm_final_g, norm_mix_2, w_in_2, conv_w,
            conv_b, dt_bias, a_log, d_skip, ssd_norm, attn_sinks, attn_norm, w_out_2, norm_ffn_2,
            w_router_group, w_router_expert, w_gate, w_up, w_down, norm_final, bucket_of_line, out):
    line_dram = nc.dram_tensor("bias_line", (HEADS, LINE), F32).ap()

    def columns(w, c0, n):
        return w[0, :, c0:c0 + n].rearrange("(k p) n -> p k n", p=P)

    def panel_source(kind, j):
        if kind in ("u", "v", "q", "k", "va", "ga", "gb"):
            at = ["u", "v", "q", "k", "va", "ga", "gb"].index(kind) * D
            return columns(w_in, at + 512 * j, 512)
        if kind in ("wo", "pg"):
            return columns({"wo": w_out, "pg": w_ple_gate}[kind], 512 * j, 512)
        if kind == "ff1":
            return columns(w_ff1, 512 * j, 512)
        if kind in ("ff2", "wo2"):
            w, rows, half = {"ff2": w_ff2, "wo2": w_out_2}[kind], D * (j // 2), 512 * (j % 2)
            return w[0, rows:rows + D, half:half + 512].rearrange("(k p) n -> p k n", p=P)
        if kind == "pp":
            return columns(w_ple_proj, 0, D)
        at = {"z": 0, "xbc": D, "q2": 2576, "kv2": 3600}[kind]
        return columns(w_in_2, at + 512 * j, 256 if kind == "kv2" else 512)

    with ExitStack() as ctx:
        def sb(name, shape, dt=F32):
            return ctx.enter_context(nc.sbuf_tensor(name, shape, dt))

        def sem(name):
            return ctx.enter_context(nc.semaphore(name))

        ring = sb("ring", [P, RING, 4096])
        x = sb("x", [P, MT, D])
        hT = sb("hT", [P, KT, S])
        areas = sb("areas", [P, 10, 2048])
        soft = sb("soft", [P, 2, 384])
        softT = sb("softT", [P, 2, 384])
        cols = sb("cols", [P, NROWS])
        ident = sb("ident", [P, P])
        upper = sb("upper", [P, P])
        above = sb("above", [P, P])
        ones = sb("ones", [P, P])
        one = sb("one", [P, 2])
        window = sb("window", [P, S])
        table = sb("table", [BUCKETS + 1, HEADS])
        stats = sb("stats", [P, 16])
        peak = sb("peak", [P, 4, 2])
        head_sum = sb("head_sum", [P, 4, 4])
        sink_e = sb("sink_e", [P, 4, 2])
        heads4 = sb("heads4", [P, 4, HEADS])
        neg_sink = sb("neg_sink", [P, HEADS])
        dtw = sb("dtw", [P, KT, HEADS])
        dts_all = sb("dts_all", [P, 16 * MT * HEADS])
        iota_i = sb("iota_i", [P, SLOTS], I32)
        iota = sb("iota", [P, SLOTS])
        count_i = sb("count_i", [P, NE + 1], I32)

        def area(n, k=1):
            return areas[:, n:n + k, :].rearrange("p a n -> p (a n)")

        def rows_area(n):
            return area(n).rearrange("p (m c) -> p m c", m=MT)

        def cols_area(n, tiles=KT):
            return area(n, tiles * S // 2048).rearrange("p (k t) -> p k t", k=tiles)

        xn = rows_area(9)
        v_rows, u_rows, qT, kT, va, sga, sgb, yb = (rows_area(0), rows_area(1), cols_area(2), cols_area(3),
                                                   rows_area(4), rows_area(5), rows_area(6), rows_area(9))
        bias = area(7, 2).rearrange("p (h j) -> p h j", h=HEADS)
        w_s = area(7)[:, 0:1024].rearrange("p (g s) -> p g s", g=GROUPS)
        w_sT = area(7)[:, 1024:2048].rearrange("p (g s) -> p g s", g=GROUPS)
        small_rows = area(5)[0:NROWS, 0:P]
        ln_vecs = rows_area(4)
        hidT = cols_area(0, FT)
        final_g = area(8)[:, 0:D]
        xg = rows_area(7)
        p_rows = area(6)[:, 0:512].rearrange("p (m c) -> p m c", m=MT)
        pT = area(6)[:, 512:1024].rearrange("p (k t) -> p k t", k=2)
        gate_rows = rows_area(5)
        q2T, xraw, xc, sz = (cols_area(0), area(1, 2)[:, 0:CT * (S + TAPS - 1)].rearrange("p (c t) -> p c t", c=CT),
                             area(3, 2)[:, 0:CT * S].rearrange("p (c t) -> p c t", c=CT), rows_area(5))
        xtok, xdt, y, att = rows_area(6), rows_area(7), rows_area(8), rows_area(9)
        k2T = area(4)[:, 1024:1536].rearrange("p (g t) -> p g t", g=2)
        v2 = area(4)[:, 1536:1792].rearrange("p (m c) -> p m c", m=MT)
        b_tok = area(4)[:, 1792:2048].rearrange("p (g n) -> p g n", g=2)
        decay = area(1).rearrange("p (h l) -> p h l", h=HEADS)
        state = area(2)[:, 0:1024]
        xde = area(2)[:, 1024:2048]
        cbm = sb("cbm_all", [P, 512])[:, :].rearrange("p (m g l) -> p m g l", m=MT, g=2)
        dts = dts_all[:, :].rearrange("p (n m h) -> p n m h", n=16, m=MT)
        attT = cols_area(0)
        t_rows = rows_area(0)
        zeros = area(4)[:, 0:512]
        gains = rows_area(5)
        routerw = area(7)[:, 0:KT * (EG + NE)].rearrange("p (k n) -> p k n", k=KT)
        xeT = area(1)[:, 0:1024].rearrange("p (k s) -> p k s", k=KT)
        h_e = area(1)[:, 1024:1536]
        heT = area(1)[:, 1536:2048].rearrange("p (c s) -> p c s", c=4)
        y_e = area(2)[:, 0:1024]
        pick = area(2)[:, 1024:1280].rearrange("p (m e s) -> p m e s", m=MT, e=2)
        pick_g = area(2)[:, 1280:1536].rearrange("p (m e s) -> p m e s", m=MT, e=2)
        put = area(2)[:, 1536:1792].rearrange("p (m t) -> p m t", m=MT)
        logits = area(3)[:, 0:144].rearrange("p (m e) -> p m e", m=MT)
        rt = area(3)[:, 144:144 + 56 * 16].rearrange("p (n m e) -> p n m e", n=56, m=MT)
        one_hot = area(3)[:, 1100:1100 + 768].rearrange("p (n m e) -> p n m e", n=6, m=MT)

        banks = [ctx.enter_context(nc.psum_tensor(f"bank{b}", [P, 512], F32)) for b in range(8)]

        x_loaded, p_loaded, rows_loaded, ws_loaded = sem("x_loaded"), sem("p_loaded"), sem("rows_loaded"), sem("ws_loaded")
        ln_loaded, table_loaded, bucket_loaded, heads_loaded = (sem("ln_loaded"), sem("table_loaded"),
                                                                sem("bucket_loaded"), sem("heads_loaded"))
        dtw_loaded, router_loaded, line_stored, bias_loaded = (sem("dtw_loaded"), sem("router_loaded"),
                                                               sem("line_stored"), sem("bias_loaded"))
        gains_loaded, out_stored = sem("gains_loaded"), sem("out_stored")
        landed = [sem(f"panel_landed{s}") for s in range(RING)]
        panel_done, emptied_a, emptied_d = sem("panel_done"), sem("emptied_by_scalar"), sem("emptied_by_vector")
        consts_made, ws_masked = sem("consts_made"), sem("ws_masked")
        act_step, dve_step, pool_step = sem("act_step"), sem("dve_step"), sem("pool_step")
        rows_turned, cols_ready, ws_turned, wsT_ready = (sem("rows_turned"), sem("cols_ready"), sem("ws_turned"),
                                                         sem("wsT_ready"))
        line_ready, line_copied, p_turned, pT_ready = sem("line_ready"), sem("line_copied"), sem("p_turned"), sem("pT_ready")
        squares, mean_ready, root_ready, rstd_ready = sem("squares"), sem("mean_ready"), sem("root_ready"), sem("rstd_ready")
        xn_a, xn_d, turned, hT_a, hT_d = sem("xn_by_scalar"), sem("xn_by_vector"), sem("turned"), sem("hT_by_scalar"), sem("hT_by_vector")
        v_mean, v_root, v_normed = sem("v_mean"), sem("v_root"), sem("v_normed")
        xg_ready = sem("xg_ready")
        table_ones, final_loaded, zeros_made, picked_g, moved = (sem("table_ones"), sem("final_loaded"), sem("zeros_made"),
                                                                 sem("picked_g"), sem("moved"))
        sgu_mixed, ya_ready = sem("sgu_mixed"), sem("ya_ready")
        scored, scores_taken, peak_ready, probs_ready = sem("scored"), sem("scores_taken"), sem("peak_ready"), sem("probs_ready")
        probs_turned, softT_ready, heads_out, heads_kept = sem("probs_turned"), sem("softT_ready"), sem("heads_out"), sem("heads_kept")
        merged, x_ready, hid_raw, hid_ready, ff_done = sem("merged"), sem("x_ready"), sem("hid_raw"), sem("hid_ready"), sem("ff_done")
        proj_done, sink_ready = sem("proj_done"), sem("sink_ready")
        dt_made, dt_in, dt_exp, dt_log, dt_ready = sem("dt_made"), sem("dt_in"), sem("dt_exp"), sem("dt_log"), sem("dt_ready")
        w_exp, conv_ready, xc_ready, pads_zero = sem("w_exp"), sem("conv_ready"), sem("xc_ready"), sem("pads_zero")
        x_turned, xtok_a, xtok_d, xdt_ready = sem("x_turned"), sem("xtok_by_scalar"), sem("xtok_by_vector"), sem("xdt_ready")
        sums_made, sums_ready, cb_made, cb_ready = sem("sums_made"), sem("sums_ready"), sem("cb_made"), sem("cb_ready")
        end_exp, seg_made, seg_ready, decay_exp, decay_ready = sem("end_exp"), sem("seg_made"), sem("seg_ready"), sem("decay_exp"), sem("decay_ready")
        diag_made, diag_taken, xde_ready, state_made, state_ready, off_made = (sem("diag_made"), sem("diag_taken"), sem("xde_ready"),
                                                                               sem("state_made"), sem("state_ready"), sem("off_made"))
        y_gated, att_ready, wo2_done = sem("y_gated"), sem("att_ready"), sem("wo2_done")
        t_ready, routed, route_max, route_exp, marks_ready, ranks_made, marks_done = (
            sem("t_ready"), sem("routed"), sem("route_max"), sem("route_exp"), sem("marks_ready"), sem("ranks_made"), sem("marks_done"))
        pair_landed = {(w, e): sem(f"{w}{e}_landed") for w in ("gate", "up", "down") for e in range(2)}
        picked, gathered, xe_a, xe_d = sem("picked"), sem("gathered"), sem("xe_by_scalar"), sem("xe_by_vector")
        gated, upped, silu_ready, he_ready = sem("gated"), sem("upped"), sem("silu_ready"), sem("he_ready")
        he_turned, heT_ready, put_turned, put_ready = sem("he_turned"), sem("heT_ready"), sem("put_turned"), sem("put_ready")
        downed, ye_a, ye_d, scattered, y_summed = sem("downed"), sem("ye_by_scalar"), sem("ye_by_vector"), sem("scattered"), sem("y_summed")
        out_ready = sem("out_ready")

        def col(name, k):
            return cols[:, ROWS[name][0] + k:ROWS[name][0] + k + 1]

        def linker(eng, step):
            count = [0]

            def link(ins):
                count[0] += 1
                ins.then_inc(step, 1)
                eng.wait_ge(step, count[0])
            return link

        def panel(p):
            kind = PANELS[p][0]
            k, n = {"pp": (2, 1024), "kv2": (8, 256)}.get(kind, (8, 512))
            return ring[:, p % RING, 0:k * n].rearrange("p (k n) -> p k n", k=k)

        def expert_panel(w, e):
            s = {"gate": 0, "up": 2, "down": 4}[w] + e
            return ring[:, s, :].rearrange("p (k n) -> p k n", k=4 if w == "down" else 8)

        TURNS = [(xn, hT, "norm_mix_g"), (yb, hT, None), (xn, hT, "norm_ffn_g"), (xn, hT, "norm_ple_g"),
                 (xn, hT, "norm_mix_2"), (att, attT, "attn_norm"), (y, hT, "ssd_norm"), (xn, hT, "norm_ffn_2")]
        T_MIX, T_MERGED, T_FFN, T_PLE, T_MIX2, T_ATT, T_SSD, T_FFN2 = range(8)
        X_MLP, X_PLE, X_OUT1, X_MIX2, X_MOE = 4, 8, 10, 14, 18
        NORM_OF = {T_MIX: 0, T_FFN: 1, T_PLE: 2, T_MIX2: 3, T_FFN2: 4}

        block = ctx.enter_context(nc.Block())

        @block.sync
        def _(sp):
            sp.dma_start(x[:, :, :], x_in[0].rearrange("(m p) c -> p m c", p=P)).then_inc(x_loaded, 16)
            for p, (kind, j) in enumerate(PANELS):
                if p >= RING:
                    sp.wait_ge(panel_done, p - RING + 1)
                sp.dma_start(panel(p), panel_source(kind, j)).then_inc(landed[p % RING], 16)
                if p == 0:
                    sp.dma_start(table[0:BUCKETS, :], rel_bias).then_inc(table_loaded, 16)
                    sp.dma_start(area(6)[0:BUCKETS + 1, 0:LINE], bucket_of_line).then_inc(bucket_loaded, 16)
                    sp.dma_start(w_s, w_sgu[0].rearrange("g t s -> t g s")).then_inc(ws_loaded, 16)
                if p == 1:
                    sp.dma_start(ln_vecs[:, 0, :], ln_v_g.to_broadcast([P, D])).then_inc(ln_loaded, 16)
                    sp.dma_start(ln_vecs[:, 1, :], ln_v_b.to_broadcast([P, D])).then_inc(ln_loaded, 16)
                if p == 5:
                    for n, v in enumerate((dt_bias, a_log, d_skip, attn_sinks)):
                        sp.dma_start(heads4[:, n, :], v.to_broadcast([P, HEADS])).then_inc(heads_loaded, 16)
                    sp.dma_start(dtw[:, :, :], columns(w_in_2, 2560, HEADS)).then_inc(dtw_loaded, 16)
            def expert_loads(i, pair, beyond):
                for w, weights, used, slot in (("gate", w_gate, gated, 0), ("up", w_up, upped, 2), ("down", w_down, downed, 4)):
                    if isinstance(i, int):
                        sp.wait_ge(panel_done, 1 + max(p for p in range(NP) if p % RING in (slot, slot + 1)))
                    else:
                        sp.wait_ge(used, i)
                    for e in range(2):
                        cond = {} if beyond is None else {"cond": tokens[e] > beyond}
                        sp.dma_start(expert_panel(w, e), weights[0, 2 * pair + e].rearrange("(k p) n -> p k n", p=P),
                                     **cond).then_inc(pair_landed[w, e], 16)

            def tokens_of(pair):
                return [sp.value_load(count_i[0:1, bass.ds(2 * pair + e, 1)], min_val=0, max_val=S) for e in range(2)]

            tokens = None
            expert_loads(0, 0, None)
            sp.wait_ge(marks_done, 1)
            fullest = sp.value_load(count_i[0:1, NE:NE + 1], min_val=0, max_val=S)
            with sp.Fori(1, PAIRS) as i:
                tokens = tokens_of(i)
                expert_loads(i, i, 0)
            with sp.If(fullest > SLOTS):
                with sp.Fori(1, PASSES) as r:
                    with sp.Fori(0, PAIRS) as j:
                        tokens = tokens_of(j)
                        expert_loads(r * PAIRS + j, j, r * SLOTS)
            sp.wait_ge(out_ready, MT)
            sp.dma_start(out[0].rearrange("(m p) c -> p m c", p=P), xn).then_inc(out_stored, 16)
            sp.wait_ge(out_stored, 16)

        @block.gpsimd
        def _(pool):
            link = linker(pool, pool_step)
            for made in (ident[:, :], window[:, :]):
                nc.gpsimd.memset(made, 0.0)
            for made in (upper[:, :], above[:, :], one[:, :], ones[:, :]):
                link(nc.gpsimd.memset(made, 1.0))
            nc.gpsimd.affine_select(out=ident[:, :], in_=ident[:, :], compare_op=ALU.not_equal, fill=1.0, base=0,
                                    pattern=[[-1, P]], channel_multiplier=1)
            nc.gpsimd.affine_select(out=upper[:, :], in_=upper[:, :], compare_op=ALU.is_ge, fill=0.0, base=0,
                                    pattern=[[1, P]], channel_multiplier=-1)
            nc.gpsimd.affine_select(out=above[:, :], in_=above[:, :], compare_op=ALU.is_gt, fill=0.0, base=0,
                                    pattern=[[1, P]], channel_multiplier=-1)
            link(nc.gpsimd.affine_select(out=window[:, :], in_=window[:, :], compare_op=ALU.is_gt, fill=MASKED, base=0,
                                         pattern=[[1, S]], channel_multiplier=-1))
            nc.gpsimd.affine_select(out=window[:, :], in_=window[:, :], compare_op=ALU.is_ge, fill=MASKED, base=P,
                                    pattern=[[-1, S]], channel_multiplier=1)
            link(nc.gpsimd.iota(iota_i[:, :], pattern=[[1, SLOTS]], base=0, channel_multiplier=0))
            nc.gpsimd.tensor_copy(iota[:, :], iota_i[:, :]).then_inc(consts_made, 1)
            pool.wait_ge(ws_loaded, 16)
            nc.gpsimd.affine_select(out=w_s, in_=w_s, compare_op=ALU.is_ge, fill=0.0, base=0,
                                    pattern=[[0, GROUPS], [-1, P]], channel_multiplier=1).then_inc(ws_masked, 1)
            pool.wait_ge(line_copied, 1)
            pool.dma_start(line_dram, soft[0:HEADS, :, :].rearrange("p a b -> p (a b)")[:, 0:LINE]).then_inc(line_stored, 16)
            pool.wait_ge(line_stored, 16)
            pool.wait_ge(sgu_mixed, 4)
            pool.dma_start(bias, bass.AP(line_dram.tensor, 0, [[1, P], [LINE, HEADS], [1, S]])).then_inc(bias_loaded, 16)
            pool.wait_ge(merged, MT)
            pool.dma_start(final_g, norm_final_g.rearrange("(a n) -> a n", a=1).to_broadcast([P, D])).then_inc(final_loaded, 16)
            pool.dma_start(p_rows, p_in[0, 0].rearrange("(m p) c -> p m c", p=P)).then_inc(p_loaded, 16)
            pool.wait_ge(rstd_ready, 5)
            for m in range(MT):
                nc.gpsimd.tensor_scalar(x[:, m, :], xg[:, m, :], stats[:, 8 + m:9 + m], 1.0, ALU.mult, ALU.mult).then_inc(x_ready, 1)
            nc.gpsimd.memset(xraw[:, :, 0:TAPS - 1], 0.0).then_inc(pads_zero, 1)
            pool.wait_ge(y_gated, 1)
            pool.dma_start(gains[:, 0, :], norm_ffn_2.to_broadcast([P, D])).then_inc(gains_loaded, 16)
            pool.dma_start(gains[:, 1, :], norm_final.rearrange("(a n) -> a n", a=1).to_broadcast([P, D])).then_inc(gains_loaded, 16)
            pool.dma_start(routerw[:, :, 0:EG], columns(w_router_group, 0, EG)).then_inc(router_loaded, 16)
            pool.dma_start(routerw[:, :, EG:], columns(w_router_expert, 0, NE)).then_inc(router_loaded, 16)
            nc.gpsimd.memset(zeros, 0.0).then_inc(zeros_made, 1)

        @block.scalar
        def _(act):
            link = linker(act, act_step)
            act_ = nc.scalar.activation
            sources = {"norm_mix_g": norm_mix_g, "norm_ffn_g": norm_ffn_g, "norm_ple_g": norm_ple_g, "b_sgu": b_sgu,
                       "norm_mix_2": norm_mix_2, "conv_w": conv_w, "conv_b": conv_b, "ssd_norm": ssd_norm,
                       "attn_norm": attn_norm, "norm_ffn_2": norm_ffn_2}
            for name, (first, n) in ROWS.items():
                src = sources[name]
                if name == "conv_w":
                    src = src[0].rearrange("j (c p) -> (j c) p", p=P)
                elif name == "b_sgu":
                    src = src[0]
                else:
                    src = src[0].rearrange("(c p) -> c p", p=P)
                act.dma_start(small_rows[first:first + n], src).then_inc(rows_loaded, 16)

            def sum_squares(src, n, squared, first=0):
                for i in range(D // n):
                    part = slice(n * i, n * i + n)
                    last = act_(squared[:, 0, part], src[:, 0, part], ACT.Square,
                                accum_out=stats[:, first + i:first + i + 1])
                last.then_inc(squares, 1)

            def load_roots():
                act_(one[:, 1:2], one[:, 0:1], ACT.Sqrt)

            norms = [0]

            def norm(t, n_stats):
                norms[0] += 1
                act.wait_ge(mean_ready, norms[0])
                act_(stats[:, 4:4 + n_stats], stats[:, 4:4 + n_stats], ACT.Sqrt).then_inc(root_ready, 1)

            def norm_x(t):
                load_roots()
                if t == T_MIX:
                    act.wait_ge(x_loaded, 16)
                elif t == T_FFN:
                    act.wait_ge(emptied_d, emptied("d", AT["wo", 1]))
                else:
                    act.wait_ge(x_ready, {T_PLE: X_MLP, T_MIX2: X_OUT1, T_FFN2: X_MIX2}[t])
                sum_squares(x, D, xn)
                norm(t, MT)
                act.wait_ge(rstd_ready, norms[0])
                act_(xn[:, 1, :], x[:, 1, :], ACT.Copy, scale=stats[:, 9:10]).then_inc(xn_a, 1)

            def turn(t):
                _, dst, gain = TURNS[t]
                for b in (1, 3):
                    act.wait_ge(turned, 4 * t + b + 1)
                    for k in (2 * b, 2 * b + 1):
                        psum = banks[b][:, S * (k % 2):S * (k % 2) + S]
                        last = act_(dst[:, k, :], psum, ACT.Copy, scale=col(gain, k) if gain else 1.0)
                    last.then_inc(hT_a, 1)

            def empty(kind, j):
                p = AT[kind, j]
                act.wait_ge(panel_done, p + 1)
                for b, engine in enumerate(EMPTIED_BY[kind]):
                    if engine != "a":
                        continue
                    bank = banks[pair_of(p) + b]
                    half = slice(512 * j, 512 * j + 512)
                    if kind in ("v", "u"):
                        ins = act_((v_rows if kind == "v" else u_rows)[:, b, half], bank[:, :], ACT.Gelu_apprx_tanh)
                    elif kind in ("ga", "gb", "pg"):
                        ins = act_({"ga": sga, "gb": sgb, "pg": gate_rows}[kind][:, b, half], bank[:, :], ACT.Sigmoid)
                    elif kind == "z":
                        ins = act_(sz[:, b, half], bank[:, :], ACT.Silu)
                    elif kind in ("q", "k", "q2"):
                        dst = {"q": qT, "k": kT, "q2": q2T}[kind][:, 4 * j + 2 * b:4 * j + 2 * b + 2, :]
                        ins = act_(dst.rearrange("p k t -> p (k t)"), bank[:, :], ACT.Copy,
                                   scale=1.0 if kind == "k" else Q_SCALE)
                    elif kind == "va":
                        ins = act_(va[:, b, half], bank[:, :], ACT.Copy)
                    elif kind == "ff1":
                        dst = hidT[:, 4 * j + 2 * b:4 * j + 2 * b + 2, :].rearrange("p k t -> p (k t)")
                        ins = act_(dst, bank[:, :], ACT.Relu)
                    elif kind == "kv2":
                        ins = act_(k2T.rearrange("p g t -> p (g t)"), bank[:, :], ACT.Copy)
                    elif kind == "xbc":
                        ins = act_(xraw[:, 4 * j + 2 * b:4 * j + 2 * b + 2, TAPS - 1:],
                                   bank[:, :].rearrange("p (c t) -> p c t", c=2), ACT.Copy)
                    ins.then_inc(emptied_a, 1)

            def head_exp(n):
                b = n % 2
                act.wait_ge(peak_ready, n + 1)
                act_(soft[:, b, 0:S], soft[:, b, 0:S], ACT.Exp, bias=peak[:, n % 4, 0:1], accum_out=head_sum[:, n % 4, 0:1])
                last = act_(soft[:, b, S:], soft[:, b, S:], ACT.Exp, bias=peak[:, n % 4, 1:2], accum_out=head_sum[:, n % 4, 1:2])
                if n >= HEADS:
                    last = act_(sink_e[:, n % 4, :], peak[:, n % 4, 0:2], ACT.Exp, bias=heads4[:, 3, n - HEADS:n - HEADS + 1])
                last.then_inc(probs_ready, 1)

            def head_turned(n):
                act.wait_ge(probs_turned, n + 1)
                if n >= 2:
                    act.wait_ge(heads_out, n - 1)
                act_(softT[:, n % 2, :], banks[6 + n % 2][:, 0:384], ACT.Copy).then_inc(softT_ready, 1)

            act.wait_ge(consts_made, 1)
            norm_x(T_MIX)
            act.wait_ge(cols_ready, 1)
            turn(T_MIX)
            for kind, j in (("v", 0), ("v", 1), ("u", 0)):
                empty(kind, j)
            act.wait_ge(v_mean, 1)
            act_(stats[:, 14:16], stats[:, 14:16], ACT.Sqrt).then_inc(v_root, 1)
            for kind, j in (("u", 1), ("q", 0), ("q", 1), ("k", 0), ("k", 1), ("va", 0), ("va", 1)):
                empty(kind, j)
            for step in range(HEADS + 2):
                if step < HEADS:
                    head_exp(step)
                if 1 <= step <= HEADS:
                    head_turned(step - 1)
                if step < HEADS and step % 4 == 3:
                    empty(("gb", "ga")[step // 8], (step // 4) % 2)
            turn(T_MERGED)
            norm_x(T_FFN)
            turn(T_FFN)
            for j in range(8):
                empty("ff1", j)
            norm_x(T_PLE)
            turn(T_PLE)
            for j in range(2):
                empty("pg", j)
            load_roots()
            act.wait_ge(x_ready, X_PLE)
            sum_squares(x, D, rows_area(3))
            act.wait_ge(xg_ready, 1)
            sum_squares(xg, D, rows_area(2), 2)
            for n in range(2):
                norms[0] += 1
                act.wait_ge(mean_ready, norms[0])
                act_(stats[:, 4 + 2 * n:6 + 2 * n], stats[:, 4 + 2 * n:6 + 2 * n], ACT.Sqrt).then_inc(root_ready, 1)
            act.wait_ge(rstd_ready, norms[0])
            act_(xn[:, 1, :], xg[:, 1, :], ACT.Copy, scale=stats[:, 11:12]).then_inc(xn_a, 1)
            turn(T_MIX2)
            for kind, j in (("q2", 0), ("q2", 1), ("kv2", 0)):
                empty(kind, j)
            act.wait_ge(dt_in, 1)
            act_(dts[:, 2], dts[:, 1], ACT.Exp, scale=-1.0).then_inc(dt_exp, 1)
            act.wait_ge(heads_loaded, 64)
            act_(heads4[:, 1, :], heads4[:, 1, :], ACT.Exp).then_inc(w_exp, 1)
            act.wait_ge(dt_in, 2)
            act_(dts[:, 4], dts[:, 3], ACT.Ln).then_inc(dt_log, 1)
            for step in range(HEADS + 2):
                if step < HEADS:
                    head_exp(HEADS + step)
                if 1 <= step <= HEADS:
                    head_turned(HEADS + step - 1)
                if step % 4 == 3 and step < HEADS:
                    empty(*(("xbc", 0), ("xbc", 1), ("xbc", 2), ("z", 0))[step // 4])
            empty("z", 1)
            for j in range(3):
                act.wait_ge(conv_ready, j + 1)
                part = xc[:, 4 * j:4 * j + 4, :].rearrange("p c t -> p (c t)")
                act_(part, part, ACT.Silu).then_inc(xc_ready, 1)
            load_roots()
            act.wait_ge(heads_kept, 2 * HEADS)
            sum_squares(att, D, rows_area(0))
            norm(T_ATT, MT)
            for b in (1, 3):
                act.wait_ge(x_turned, b + 1)
                act_(xtok[:, b // 2, 512:1024], banks[b][:, :], ACT.Copy).then_inc(xtok_a, 1)
            act.wait_ge(sums_ready, 1)
            act_(dts[:, 8], dts[:, 6], ACT.Exp)
            act_(dts[:, 9, 0], dts[:, 7, 0], ACT.Exp).then_inc(end_exp, 1)
            turn(T_ATT)
            for n in range(8):
                act.wait_ge(seg_ready, n + 1)
                part = decay[:, 4 * (n % 4):4 * (n % 4) + 4, :].rearrange("p h l -> p (h l)")
                act_(part, part, ACT.Exp).then_inc(decay_exp, 1)
            act.wait_ge(state_made, 1)
            act_(state[:, 0:512], banks[0][:, :], ACT.Copy)
            act_(state[:, 512:1024], banks[1][:, :], ACT.Copy).then_inc(state_ready, 1)
            load_roots()
            act.wait_ge(y_gated, 1)
            sum_squares(y, D // SSD_G, xtok)
            norm(T_SSD, 4)
            turn(T_SSD)
            norm_x(T_FFN2)
            turn(T_FFN2)
            act.wait_ge(route_max, 1)
            act_(rt[:, 3], rt[:, 2], ACT.Exp)
            act_(rt[:, 13, :, 0:1], rt[:, 12, :, 0:1], ACT.Exp).then_inc(route_exp, 1)
            act.wait_ge(marks_done, 1)
            fullest = act.value_load(count_i[0:1, NE:NE + 1], min_val=0, max_val=S)

            def experts(i):
                act.wait_ge(gathered, 2 * i + 1)
                act_(xeT[:, 0:4, :].rearrange("p k s -> p (k s)"), banks[0][:, :], ACT.Copy).then_inc(xe_a, 1)
                act.wait_ge(gated, i + 1)
                act_(h_e, banks[2][:, :], ACT.Silu).then_inc(silu_ready, 1)
                act.wait_ge(he_turned, i + 1)
                act_(heT.rearrange("p c s -> p (c s)"), banks[0][:, :], ACT.Copy).then_inc(heT_ready, 1)
                act.wait_ge(downed, i + 1)
                act_(y_e[:, 0:512], banks[2][:, :], ACT.Copy).then_inc(ye_a, 1)

            with act.Fori(0, PAIRS) as i:
                experts(i)
            with act.If(fullest > SLOTS):
                with act.Fori(1, PASSES) as r:
                    with act.Fori(0, PAIRS) as j:
                        experts(r * PAIRS + j)
            load_roots()
            act.wait_ge(x_ready, X_MOE)
            sum_squares(x, D, xn)
            norm(None, MT)

        @block.tensor
        def _(pe):
            mm, turn_tile = nc.tensor.matmul, nc.tensor.transpose

            def banks_empty(p):
                for engine, s in (("a", emptied_a), ("d", emptied_d)):
                    if emptied(engine, p):
                        pe.wait_ge(s, emptied(engine, p))

            def turn(t):
                src, _, _ = TURNS[t]
                for b in range(4):
                    for k in (2 * b, 2 * b + 1):
                        for m in range(MT):
                            at = S * (k % 2) + P * m
                            last = turn_tile(banks[b][:, at:at + P], src[:, m, P * k:P * k + P], ident[:, :])
                    last.then_inc(turned, 1)

            def normed_turn(t, p):
                pe.wait_ge(xn_d, NORM_OF[t] + 1)
                pe.wait_ge(xn_a, NORM_OF[t] + 1)
                if p is not None:
                    banks_empty(p)
                turn(t)

            def hT_ready(t):
                pe.wait_ge(hT_d, 2 * t + 2)
                pe.wait_ge(hT_a, 2 * t + 2)

            def quarter(kind, j, c):
                p = AT[kind, j]
                w = panel(p)
                if c == 0:
                    if before_in_pair(p) is not None:
                        banks_empty(before_in_pair(p))
                    pe.wait_ge(landed[p % RING], 16 * (p // RING + 1))
                b0 = pair_of(p)
                if kind in ("q", "k", "q2", "ff1", "xbc"):
                    for k in range(KT):
                        last = mm(banks[b0 + c // 2][:, S * (c % 2):S * (c % 2) + S], w[:, k, P * c:P * c + P],
                                  hT[:, k, :], start=(k == 0), stop=(k == KT - 1))
                else:
                    for k in (2 * c, 2 * c + 1):
                        for m in range(MT):
                            last = mm(banks[b0 + m][:, :], hT[:, k, P * m:P * m + P], w[:, k, :],
                                      start=(k == 0), stop=(k == KT - 1))
                if c == 3:
                    last.then_inc(panel_done, 1)

            def whole(kind, j):
                for c in range(4):
                    quarter(kind, j, c)

            def scores(n, q, k, k_tile):
                h = n % HEADS
                if n >= 2:
                    pe.wait_ge(scores_taken, n - 1)
                r = slice(DH * (h % 2), DH * (h % 2) + DH)
                bank = banks[4 + n % 2]
                mm(bank[:, 0:S], q[r, h // 2, P:S], k[r, k_tile, :], start=True, stop=True)
                mm(bank[:, S:S + P], q[r, h // 2, 0:P], k[r, k_tile, 0:P], start=True, stop=True).then_inc(scored, 1)

            def turn_probs(n):
                pe.wait_ge(probs_ready, n + 1)
                if n >= 2:
                    pe.wait_ge(heads_kept, n - 1)
                for c in range(3):
                    last = turn_tile(banks[6 + n % 2][:, P * c:P * c + P], soft[:, n % 2, P * c:P * c + P], ident[:, :])
                last.then_inc(probs_turned, 1)

            def values(n, v, c0):
                pe.wait_ge(softT_ready, n + 1)
                bank, b = banks[6 + n % 2], n % 2
                mm(bank[:, 384:448], softT[:, b, 256:384], v[:, 0, c0:c0 + DH], start=True, stop=True)
                mm(bank[:, 448:512], softT[:, b, 0:128], v[:, 0, c0:c0 + DH], start=True, stop=False)
                mm(bank[:, 448:512], softT[:, b, 128:256], v[:, 1, c0:c0 + DH], start=False, stop=True).then_inc(heads_out, 1)

            pe.wait_ge(consts_made, 1)
            pe.wait_ge(rows_loaded, 16 * len(ROWS))
            turn_tile(banks[4][:, 0:NROWS], small_rows, ident[0:NROWS, 0:NROWS]).then_inc(rows_turned, 1)
            normed_turn(T_MIX, None)
            hT_ready(T_MIX)
            whole("v", 0)
            pe.wait_ge(table_loaded, 16)
            pe.wait_ge(bucket_loaded, 16)
            pe.wait_ge(table_ones, 1)
            mm(banks[5][0:HEADS, 0:LINE], table[:, :], area(6)[0:BUCKETS + 1, 0:LINE], start=True, stop=True)\
                .then_inc(line_ready, 1)
            pe.wait_ge(ws_masked, 1)
            for g in range(GROUPS):
                last = turn_tile(banks[6 + g // 4][:, P * (g % 4):P * (g % 4) + P], w_s[:, g, :], ident[:, :])
            last.then_inc(ws_turned, 1)
            for kind, j in (("v", 1), ("u", 0), ("u", 1), ("q", 0), ("q", 1)):
                whole(kind, j)
            pe.wait_ge(wsT_ready, 1)
            pe.wait_ge(v_normed, 2)
            pe.wait_ge(cols_ready, 1)
            pe.wait_ge(line_copied, 1)
            for m in range(MT):
                for half in range(2):
                    for g in range(4 * half, 4 * half + 4):
                        last = mm(banks[4 + 2 * m + half][:, P * (g % 4):P * (g % 4) + P], w_sT[:, g, :],
                                  v_rows[:, m, P * g:P * g + P], start=True, stop=True)
                    last.then_inc(sgu_mixed, 1)
            for kind, j in (("k", 0), ("k", 1), ("va", 0), ("va", 1)):
                whole(kind, j)
            banks_empty(AT["va", 1])
            pe.wait_ge(ya_ready, 4)
            for step in range(HEADS + 2):
                if step < HEADS:
                    scores(step, qT, kT, step // 2)
                    quarter(("gb", "ga")[step // 8], (step // 4) % 2, step % 4)
                if 1 <= step <= HEADS:
                    turn_probs(step - 1)
                if step >= 2:
                    values(step - 2, va, DH * (step - 2))
            banks_empty(AT["ga", 1])
            pe.wait_ge(merged, 2)
            turn(T_MERGED)
            hT_ready(T_MERGED)
            for j in range(2):
                whole("wo", j)
            normed_turn(T_FFN, AT["wo", 1])
            hT_ready(T_FFN)
            for j in range(8):
                whole("ff1", j)
            for j in range(8):
                p = AT["ff2", j]
                pe.wait_ge(landed[p % RING], 16 * (p // RING + 1))
                pe.wait_ge(hid_ready, 4 * (j // 2) + 4)
                for k in range(KT):
                    for m in range(MT):
                        last = mm(banks[4 + 2 * m + j % 2][:, :], hidT[:, KT * (j // 2) + k, P * m:P * m + P],
                                  panel(p)[:, k, :], start=(j < 2 and k == 0), stop=(j >= 6 and k == KT - 1))
                last.then_inc(panel_done, 1)
            normed_turn(T_PLE, AT["ff1", 7])
            pe.wait_ge(x_ready, X_MLP)
            pe.wait_ge(p_loaded, 16)
            for k in range(2):
                for m in range(MT):
                    last = turn_tile(banks[4][:, S * k + P * m:S * k + P * m + P], p_rows[:, m, P * k:P * k + P], ident[:, :])
            last.then_inc(p_turned, 1)
            p = AT["pp", 0]
            pe.wait_ge(landed[p % RING], 16 * (p // RING + 1))
            pe.wait_ge(pT_ready, 1)
            for half in range(2):
                for k in range(2):
                    for m in range(MT):
                        last = mm(banks[4 + 2 * m + half][:, :], pT[:, k, P * m:P * m + P],
                                  panel(p)[:, k, 512 * half:512 * half + 512], start=(k == 0), stop=(k == 1))
            last.then_inc(panel_done, 1)
            hT_ready(T_PLE)
            for j in range(2):
                whole("pg", j)
            normed_turn(T_MIX2, AT["pg", 1])
            hT_ready(T_MIX2)
            pe.wait_ge(x_ready, X_PLE)
            pe.wait_ge(dtw_loaded, 16)
            for m in range(MT):
                for k in range(KT):
                    last = mm(banks[4][:, HEADS * m:HEADS * m + HEADS], hT[:, k, P * m:P * m + P], dtw[:, k, :],
                              start=(k == 0), stop=(k == KT - 1))
            last.then_inc(dt_made, 1)
            for j in range(2):
                whole("q2", j)
            p = AT["kv2", 0]
            w, b0 = panel(p), pair_of(p)
            banks_empty(before_in_pair(p))
            pe.wait_ge(landed[p % RING], 16 * (p // RING + 1))
            for g in range(2):
                for k in range(KT):
                    for half in range(2):
                        mm(banks[b0][DH * half:DH * half + DH, S * g:S * g + S], w[:, k, DH * g:DH * g + DH],
                           hT[:, k, :], start=(k == 0), stop=(k == KT - 1))
            for m in range(MT):
                for k in range(KT):
                    last = mm(banks[b0 + 1][:, P * m:P * m + P], hT[:, k, P * m:P * m + P], w[:, k, P:S],
                              start=(k == 0), stop=(k == KT - 1))
            last.then_inc(panel_done, 1)
            banks_empty(p)
            pe.wait_ge(dt_in, 1)
            for step in range(HEADS + 2):
                if step < HEADS:
                    scores(HEADS + step, q2T, k2T, step // 8)
                    quarter(*(("xbc", 0), ("xbc", 1), ("xbc", 2), ("z", 0))[step // 4], step % 4)
                if 1 <= step <= HEADS:
                    turn_probs(HEADS + step - 1)
                if step >= 2:
                    values(HEADS + step - 2, v2, DH * ((step - 2) // 8))
            whole("z", 1)
            banks_empty(AT["z", 1])

            def project_out(j, src, first, last_one, quarters=range(4)):
                p = AT["wo2", j]
                if quarters[0] == 0:
                    pe.wait_ge(landed[p % RING], 16 * (p // RING + 1))
                for k in (k for c in quarters for k in (2 * c, 2 * c + 1)):
                    for m in range(MT):
                        ins = mm(banks[4 + 2 * m + j % 2][:, :], src[:, k, P * m:P * m + P], panel(p)[:, k, :],
                                 start=(first and k == 0), stop=(last_one and k == KT - 1))
                if quarters[-1] == 3:
                    ins.then_inc(panel_done, 1)

            pe.wait_ge(xc_ready, 3)
            for m in range(MT):
                for half in range(2):
                    for c in range(4):
                        last = turn_tile(banks[2 * m + half][:, P * c:P * c + P], xc[:, 4 * half + c, P * m:P * m + P],
                                         ident[:, :])
                    last.then_inc(x_turned, 1)
            pe.wait_ge(heads_kept, 2 * HEADS)
            pe.wait_ge(xtok_d, 2)
            pe.wait_ge(xtok_a, 2)
            pe.wait_ge(dt_ready, 1)
            a = dts[:, 5]
            for m in range(MT):
                mm(banks[0][:, HEADS * m:HEADS * m + HEADS], upper[:, :], a[:, m, :], start=True, stop=True)
            mm(banks[0][:, 32:48], ones[:, :], a[:, 0, :], start=True, stop=True)
            for g in range(SSD_G):
                last = turn_tile(banks[0][:, P + P * g:P + P * g + P], xc[:, 8 + g, 0:P], ident[:, :])
            last.then_inc(sums_made, 1)
            for m in range(MT):
                for g in range(SSD_G):
                    last = mm(banks[1][:, 256 * m + P * g:256 * m + P * g + P], xc[:, 8 + g, P * m:P * m + P],
                              xc[:, 10 + g, P * m:P * m + P], start=True, stop=True)
            last.then_inc(cb_made, 1)
            pe.wait_ge(sums_ready, 1)
            pe.wait_ge(cb_ready, 1)
            pe.wait_ge(att_ready, 1)
            turn(T_ATT)
            hT_ready(T_ATT)

            def diagonal(m):
                pe.wait_ge(xdt_ready, 1)
                if m:
                    pe.wait_ge(diag_taken, m)
                for h in range(HEADS):
                    if h % 4 == 0:
                        pe.wait_ge(decay_ready, 4 * m + h // 4 + 1)
                    last = mm(banks[2 + h // 8][:, DH * (h % 8):DH * (h % 8) + DH], decay[:, h, :],
                              xdt[:, m, DH * h:DH * h + DH], start=True, stop=True)
                last.then_inc(diag_made, 1)

            for m in range(MT):
                for q in range(4):
                    n = 4 * m + q
                    if n >= 2:
                        pe.wait_ge(seg_ready, n - 1)
                    for h in range(4):
                        last = mm(banks[n % 2][:, P * h:P * h + P], a[:, m, 4 * q + h:4 * q + h + 1].to_broadcast([P, P]),
                                  upper[:, :], start=True, stop=True)
                    last.then_inc(seg_made, 1)
                    if q % 2:
                        project_out(2, attT, True, False, range(2 * m + q // 2, 2 * m + q // 2 + 1))
                diagonal(m)
            pe.wait_ge(xde_ready, 1)
            pe.wait_ge(seg_ready, 8)
            for g in range(SSD_G):
                last = mm(banks[g][:, :], b_tok[:, g, :], xde[:, 512 * g:512 * g + 512], start=True, stop=True)
            last.then_inc(state_made, 1)
            pe.wait_ge(state_ready, 1)
            pe.wait_ge(diag_taken, 2)
            for g in range(SSD_G):
                last = mm(banks[2 + g][:, :], xc[:, 10 + g, P:S], state[:, 512 * g:512 * g + 512], start=True, stop=True)
            last.then_inc(off_made, 1)
            project_out(3, attT, True, False)
            pe.wait_ge(y_gated, 2)
            turn(T_SSD)
            hT_ready(T_SSD)
            for j in range(2):
                project_out(j, hT, False, True)
            normed_turn(T_FFN2, None)
            hT_ready(T_FFN2)
            pe.wait_ge(router_loaded, 32)
            for m in range(MT):
                for k in range(KT):
                    last = mm(banks[0][:, 72 * m:72 * m + 72], hT[:, k, P * m:P * m + P], routerw[:, k, :],
                              start=(k == 0), stop=(k == KT - 1))
            last.then_inc(routed, 1)
            pe.wait_ge(marks_ready, 1)
            marks = one_hot[:, 2]
            mm(banks[1][:, 0:NE], above[:, :], marks[:, 0, :], start=True, stop=True)
            mm(banks[1][:, NE:2 * NE], ones[:, :], marks[:, 0, :], start=True, stop=False)
            mm(banks[1][:, NE:2 * NE], above[:, :], marks[:, 1, :], start=False, stop=True)
            mm(banks[1][:, 2 * NE:3 * NE], ones[:, :], marks[:, 0, :], start=True, stop=False)
            mm(banks[1][:, 2 * NE:3 * NE], ones[:, :], marks[:, 1, :], start=False, stop=True).then_inc(ranks_made, 1)
            pe.wait_ge(marks_done, 1)
            fullest = pe.value_load(count_i[0:1, NE:NE + 1], min_val=0, max_val=S)
            pe.wait_ge(zeros_made, 1)
            for b in range(4):
                mm(banks[4 + b][:, :], zeros[:, 0:P], zeros, start=True, stop=False)

            def experts(i):
                pe.wait_ge(picked, i + 1)
                for b in range(2):
                    for k in range(4):
                        for m in range(MT):
                            last = mm(banks[b][:, P * k:P * k + P], t_rows[:, m, P * (4 * b + k):P * (4 * b + k) + P],
                                      pick[:, m, :, :].rearrange("p e s -> p (e s)"), start=(m == 0), stop=(m == MT - 1))
                    last.then_inc(gathered, 1)
                pe.wait_ge(xe_a, i + 1)
                pe.wait_ge(xe_d, i + 1)
                for w, bank, done in (("gate", banks[2], gated), ("up", banks[3], upped)):
                    for e in range(2):
                        pe.wait_ge(pair_landed[w, e], 16 * (i + 1))
                    for k in range(KT):
                        for e in range(2):
                            last = mm(bank[SLOTS * e:SLOTS * e + SLOTS, :], xeT[:, k, SLOTS * e:SLOTS * e + SLOTS],
                                      expert_panel(w, e)[:, k, :], start=(k == 0), stop=(k == KT - 1))
                    last.then_inc(done, 1)
                pe.wait_ge(picked_g, i + 1)
                for m in range(MT):
                    last = turn_tile(banks[1][:, P * m:P * m + P], pick_g[:, m, :, :].rearrange("p e s -> p (e s)"),
                                     ident[:, :])
                last.then_inc(put_turned, 1)
                pe.wait_ge(he_ready, i + 1)
                for c in range(4):
                    last = turn_tile(banks[0][:, P * c:P * c + P], h_e[:, P * c:P * c + P], ident[:, :])
                last.then_inc(he_turned, 1)
                pe.wait_ge(heT_ready, i + 1)
                for e in range(2):
                    pe.wait_ge(pair_landed["down", e], 16 * (i + 1))
                for c in range(4):
                    for half in range(2):
                        for e in range(2):
                            last = mm(banks[2 + half][SLOTS * e:SLOTS * e + SLOTS, :], heT[:, c, SLOTS * e:SLOTS * e + SLOTS],
                                      expert_panel("down", e)[:, c, 512 * half:512 * half + 512],
                                      start=(c == 0), stop=(c == 3))
                last.then_inc(downed, 1)
                pe.wait_ge(put_ready, i + 1)
                pe.wait_ge(ye_a, i + 1)
                pe.wait_ge(ye_d, i + 1)
                for m in range(MT):
                    for half in range(2):
                        last = mm(banks[4 + 2 * m + half][:, :], put[:, m, :], y_e[:, 512 * half:512 * half + 512],
                                  start=False, stop=False)
                last.then_inc(scattered, 1)

            with pe.Fori(0, PAIRS) as i:
                experts(i)
            with pe.If(fullest > SLOTS):
                with pe.Fori(1, PASSES) as r:
                    with pe.Fori(0, PAIRS) as j:
                        experts(r * PAIRS + j)
            for b in range(4):
                last = mm(banks[4 + b][:, :], zeros[:, 0:P], zeros, start=False, stop=True)
            last.then_inc(y_summed, 1)

        @block.vector
        def _(dve):
            link = linker(dve, dve_step)
            tt, ts, stt = nc.vector.tensor_tensor, nc.vector.tensor_scalar, nc.vector.scalar_tensor_tensor
            copy, recip = nc.vector.tensor_copy, nc.vector.reciprocal
            norms = [0]

            def sum_squares(src, n, squared, first=1):
                for i in range(D // n):
                    part = slice(n * i, n * i + n)
                    last = nc.vector.tensor_tensor_reduce(squared[:, 1, part], src[:, 1, part], src[:, 1, part], 1.0, 0.0,
                                                          ALU.mult, ALU.add, stats[:, first + i:first + i + 1])
                link(last)

            def rstd(n_stats, width):
                norms[0] += 1
                dve.wait_ge(squares, norms[0])
                ts(stats[:, 4:4 + n_stats], stats[:, 0:n_stats], 1.0 / width, EPS, ALU.mult, ALU.add).then_inc(mean_ready, 1)
                dve.wait_ge(root_ready, norms[0])
                recip(stats[:, 8:8 + n_stats], stats[:, 4:4 + n_stats]).then_inc(rstd_ready, 1)
                dve.wait_ge(rstd_ready, norms[0])

            def norm_x(t):
                if t == T_MIX:
                    dve.wait_ge(x_loaded, 16)
                elif t == T_FFN:
                    dve.wait_ge(emptied_d, emptied("d", AT["wo", 1]))
                else:
                    dve.wait_ge(x_ready, {T_PLE: X_MLP, T_FFN2: X_MIX2}[t])
                sum_squares(x, D, xn)
                rstd(MT, D)
                ts(xn[:, 0, :], x[:, 0, :], stats[:, 8:9], None, ALU.mult).then_inc(xn_d, 1)

            def turn(t):
                _, dst, gain = TURNS[t]
                for b in (0, 2):
                    dve.wait_ge(turned, 4 * t + b + 1)
                    for k in (2 * b, 2 * b + 1):
                        psum = banks[b][:, S * (k % 2):S * (k % 2) + S]
                        if gain:
                            last = ts(dst[:, k, :], psum, col(gain, k), None, ALU.mult)
                        else:
                            last = copy(dst[:, k, :], psum)
                    last.then_inc(hT_d, 1)

            def empty(kind, j):
                p = AT[kind, j]
                dve.wait_ge(panel_done, p + 1)
                for b, engine in enumerate(EMPTIED_BY[kind]):
                    if engine != "d":
                        continue
                    bank = banks[pair_of(p) + b]
                    half = slice(512 * j, 512 * j + 512)
                    if kind in ("q", "k", "q2"):
                        dst = {"q": qT, "k": kT, "q2": q2T}[kind][:, 4 * j + 2 * b:4 * j + 2 * b + 2, :]
                        ins = ts(dst.rearrange("p k t -> p (k t)"), bank[:, :], 1.0 if kind == "k" else Q_SCALE, None, ALU.mult)
                    elif kind == "va":
                        ins = copy(va[:, b, half], bank[:, :])
                    elif kind == "wo":
                        ins = tt(x[:, b, half], bank[:, :], x[:, b, half], ALU.add)
                    elif kind == "kv2":
                        ins = copy(v2.rearrange("p m c -> p (m c)"), bank[:, 0:S])
                    elif kind == "xbc":
                        ins = copy(xraw[:, 4 * j + 2 * b:4 * j + 2 * b + 2, TAPS - 1:],
                                   bank[:, :].rearrange("p (c t) -> p c t", c=2))
                    ins.then_inc(emptied_d, 1)

            def head_scores(n):
                b, h, bank = n % 2, n % HEADS, banks[4 + n % 2]
                dve.wait_ge(scored, n + 1)
                if n >= 2:
                    dve.wait_ge(probs_turned, n - 1)
                mask = bias[:, h, ::-1] if n < HEADS else window[:, :]
                own = bias[:, h, P - 1::-1] if n < HEADS else window[:, P:S]
                tt(soft[:, b, 0:S], bank[:, 0:S], mask, ALU.add)
                tt(soft[:, b, S:384], bank[:, S:384], own, ALU.add).then_inc(scores_taken, 1)
                dve.wait_ge(scores_taken, n + 1)
                nc.vector.tensor_reduce(peak[:, n % 4, 0:1], soft[:, b, 0:S], AX_X, ALU.max, negate=True)
                last = nc.vector.tensor_reduce(peak[:, n % 4, 1:2], soft[:, b, S:384], AX_X, ALU.max, negate=True)
                if n >= HEADS:
                    link(last)
                    last = ts(peak[:, n % 4, 0:2], peak[:, n % 4, 0:2], neg_sink[:, h:h + 1], None, ALU.min)
                last.then_inc(peak_ready, 1)

            def head_output(n, dst):
                b, h = n % 2, n % HEADS
                dve.wait_ge(probs_ready, n + 1)
                if n >= HEADS:
                    link(tt(head_sum[:, n % 4, 0:2], head_sum[:, n % 4, 0:2], sink_e[:, n % 4, :], ALU.add))
                link(recip(head_sum[:, n % 4, 2:4], head_sum[:, n % 4, 0:2]))
                dve.wait_ge(heads_out, n + 1)
                bank = banks[6 + b]
                ts(dst[:, 0, DH * h:DH * h + DH], bank[:, 384:448], head_sum[:, n % 4, 3:4], None, ALU.mult)
                ts(dst[:, 1, DH * h:DH * h + DH], bank[:, 448:512], head_sum[:, n % 4, 2:3], None, ALU.mult).then_inc(heads_kept, 1)

            nc.vector.memset(table[BUCKETS:BUCKETS + 1, :], 1.0).then_inc(table_ones, 1)
            dve.wait_ge(rows_turned, 1)
            copy(cols[:, :], banks[4][:, 0:NROWS]).then_inc(cols_ready, 1)
            dve.wait_ge(cols_ready, 1)
            norm_x(T_MIX)
            turn(T_MIX)
            dve.wait_ge(line_ready, 1)
            copy(soft[0:HEADS, :, :].rearrange("p a b -> p (a b)")[:, 0:LINE], banks[5][0:HEADS, :]).then_inc(line_copied, 1)
            dve.wait_ge(ws_turned, 1)
            copy(w_sT[:, 0:4, :].rearrange("p g t -> p (g t)"), banks[6][:, :])
            copy(w_sT[:, 4:8, :].rearrange("p g t -> p (g t)"), banks[7][:, :]).then_inc(wsT_ready, 1)
            dve.wait_ge(emptied_a, emptied("a", AT["v", 1]))
            for m in range(MT):
                vm, mean, var = v_rows[:, m, :], stats[:, 12 + m:13 + m], stats[:, 14 + m:15 + m]
                link(nc.vector.tensor_reduce(mean, vm, AX_X, ALU.add))
                link(ts(mean, mean, -1.0 / D, None, ALU.mult))
                link(ts(vm, vm, mean, None, ALU.add))
                link(tt(xn[:, m, :], vm, vm, ALU.mult))
                link(nc.vector.tensor_reduce(var, xn[:, m, :], AX_X, ALU.add))
            ts(stats[:, 14:16], stats[:, 14:16], 1.0 / D, EPS, ALU.mult, ALU.add).then_inc(v_mean, 1)
            dve.wait_ge(ln_loaded, 32)
            dve.wait_ge(v_root, 1)
            link(recip(stats[:, 14:16], stats[:, 14:16]))
            for m in range(MT):
                vm = v_rows[:, m, :]
                link(stt(vm, vm, stats[:, 14 + m:15 + m], ln_vecs[:, 0, :], ALU.mult, ALU.mult))
                tt(vm, vm, ln_vecs[:, 1, :], ALU.add).then_inc(v_normed, 1)
            for j in range(2):
                empty("q", j)
            dve.wait_ge(emptied_a, emptied("a", AT["u", 1]))
            for m in range(MT):
                for half in range(2):
                    dve.wait_ge(sgu_mixed, 2 * m + half + 1)
                    for g in range(4 * half, 4 * half + 4):
                        u = u_rows[:, m, P * g:P * g + P]
                        last = stt(u, banks[4 + 2 * m + half][:, P * (g % 4):P * (g % 4) + P], col("b_sgu", g), u,
                                   ALU.add, ALU.mult)
                    last.then_inc(ya_ready, 1)
            for kind in ("k", "va"):
                for j in range(2):
                    empty(kind, j)
            dve.wait_ge(bias_loaded, 16)
            for step in range(HEADS + 2):
                if step < HEADS:
                    head_scores(step)
                if step >= 2:
                    head_output(step - 2, yb)
            dve.wait_ge(emptied_a, emptied("a", AT["ga", 1]))
            dve.wait_ge(heads_kept, HEADS)
            dve.wait_ge(ya_ready, 4)
            for m in range(MT):
                tt(u_rows[:, m, :], u_rows[:, m, :], sga[:, m, :], ALU.mult)
                link(tt(yb[:, m, :], yb[:, m, :], sgb[:, m, :], ALU.mult))
                tt(yb[:, m, :], yb[:, m, :], u_rows[:, m, :], ALU.add).then_inc(merged, 1)
            turn(T_MERGED)
            for j in range(2):
                empty("wo", j)
            norm_x(T_FFN)
            turn(T_FFN)
            for j in range(8):
                dve.wait_ge(emptied_a, emptied("a", AT["ff1", j]))
                for b in range(2):
                    part = hidT[:, 4 * j + 2 * b:4 * j + 2 * b + 2, :].rearrange("p k t -> p (k t)")
                    tt(part, part, part, ALU.mult).then_inc(hid_ready, 1)
            dve.wait_ge(panel_done, AT["ff2", 7] + 1)
            for b in range(4):
                part = x[:, b // 2, 512 * (b % 2):512 * (b % 2) + 512]
                tt(part, banks[4 + b][:, :], part, ALU.add).then_inc(x_ready, 1)
            norm_x(T_PLE)
            turn(T_PLE)
            dve.wait_ge(p_turned, 1)
            copy(pT.rearrange("p k t -> p (k t)"), banks[4][:, :]).then_inc(pT_ready, 1)
            for m in range(MT):
                for half in range(2):
                    g = gate_rows[:, m, 512 * half:512 * half + 512]
                    part = x[:, m, 512 * half:512 * half + 512]
                    dve.wait_ge(emptied_a, emptied("a", AT["pg", 1]))
                    link(tt(g, banks[4 + 2 * m + half][:, :], g, ALU.mult))
                    tt(part, part, g, ALU.add).then_inc(x_ready, 1)
            dve.wait_ge(x_ready, X_PLE)
            dve.wait_ge(final_loaded, 16)
            tt(xg[:, 0, :], x[:, 0, :], final_g, ALU.mult).then_inc(xg_ready, 1)
            tt(xg[:, 1, :], x[:, 1, :], final_g, ALU.mult).then_inc(xg_ready, 1)
            sum_squares(x, D, rows_area(3))
            dve.wait_ge(xg_ready, 2)
            sum_squares(xg, D, rows_area(2), 3)
            rstd(MT, D)
            r1, r2 = stats[:, 8:10], stats[:, 10:12]
            norms[0] += 1
            dve.wait_ge(squares, norms[0])
            link(tt(stats[:, 6:8], stats[:, 2:4], r1, ALU.mult))
            link(tt(stats[:, 6:8], stats[:, 6:8], r1, ALU.mult))
            ts(stats[:, 6:8], stats[:, 6:8], 1.0 / D, EPS, ALU.mult, ALU.add).then_inc(mean_ready, 1)
            dve.wait_ge(root_ready, norms[0])
            link(recip(r2, stats[:, 6:8]))
            tt(r2, r2, r1, ALU.mult).then_inc(rstd_ready, 1)
            dve.wait_ge(rstd_ready, norms[0])
            ts(xn[:, 0, :], xg[:, 0, :], r2[:, 0:1], None, ALU.mult).then_inc(xn_d, 1)
            turn(T_MIX2)
            for j in range(2):
                empty("q2", j)
            empty("kv2", 0)
            dve.wait_ge(heads_loaded, 64)
            dve.wait_ge(dt_made, 1)
            link(tt(dts[:, 0], banks[4][:, 0:32].rearrange("p (m h) -> p m h", m=MT),
                    heads4[:, 0:1, :].to_broadcast([P, MT, HEADS]), ALU.add))
            stt(dts[:, 1], dts[:, 0], -1.0, dts[:, 0], ALU.mult, ALU.max).then_inc(dt_in, 1)
            ts(neg_sink[:, :], heads4[:, 3, :], -1.0, None, ALU.mult).then_inc(sink_ready, 1)
            dve.wait_ge(sink_ready, 1)
            dve.wait_ge(dt_exp, 1)
            ts(dts[:, 3], dts[:, 2], 1.0, None, ALU.add).then_inc(dt_in, 1)
            dve.wait_ge(dt_in, 2)
            link(ts(dts[:, 10], dts[:, 3], 1.0, None, ALU.subtract))
            link(ts(dts[:, 11], dts[:, 10], 0.0, None, ALU.is_equal))
            dve.wait_ge(dt_log, 1)
            tt(dts[:, 12], dts[:, 4], dts[:, 11], ALU.add)
            link(tt(dts[:, 10], dts[:, 10], dts[:, 11], ALU.add))
            link(recip(dts[:, 13], dts[:, 10]))
            link(tt(dts[:, 12], dts[:, 12], dts[:, 13], ALU.mult))
            link(tt(dts[:, 12], dts[:, 12], dts[:, 2], ALU.mult))
            link(ts(dts[:, 13], dts[:, 0], 0.0, None, ALU.max))
            link(tt(dts[:, 0], dts[:, 12], dts[:, 13], ALU.add))
            dve.wait_ge(w_exp, 1)
            stt(dts[:, 5], dts[:, 0], -1.0, heads4[:, 1:2, :].to_broadcast([P, MT, HEADS]), ALU.mult, ALU.mult)\
                .then_inc(dt_ready, 1)

            def conv(j):
                dve.wait_ge(emptied_a, emptied("a", AT["xbc", j]))
                dve.wait_ge(emptied_d, emptied("d", AT["xbc", j]))
                if j == 0:
                    dve.wait_ge(pads_zero, 1)
                for c in range(4 * j, 4 * j + 4):
                    last = ts(xc[:, c, :], xraw[:, c, 3:3 + S], col("conv_w", 3 * CT + c), col("conv_b", c), ALU.mult, ALU.add)
                for tap in range(TAPS - 1):
                    link(last)
                    for c in range(4 * j, 4 * j + 4):
                        last = stt(xc[:, c, :], xraw[:, c, tap:tap + S], col("conv_w", tap * CT + c), xc[:, c, :],
                                   ALU.mult, ALU.add)
                last.then_inc(conv_ready, 1)

            for step in range(HEADS + 2):
                if step < HEADS:
                    head_scores(HEADS + step)
                if step >= 2:
                    head_output(HEADS + step - 2, att)
                if step % 4 == 3 and step < 12:
                    empty("xbc", step // 4)
                if step in (5, 9, 13):
                    conv((step - 5) // 4)
            dve.wait_ge(heads_kept, 2 * HEADS)
            sum_squares(att, D, rows_area(0))
            rstd(MT, D)
            for m in range(MT):
                last = ts(att[:, m, :], att[:, m, :], stats[:, 8 + m:9 + m], None, ALU.mult)
            last.then_inc(att_ready, 1)
            for b in (0, 2):
                dve.wait_ge(x_turned, b + 1)
                copy(xtok[:, b // 2, 0:512], banks[b][:, :]).then_inc(xtok_d, 1)
            dve.wait_ge(xtok_a, 2)
            dve.wait_ge(xtok_d, 2)
            by_head = lambda rows: rows.rearrange("p (h d) -> p h d", h=HEADS)
            spread = lambda v: v.unsqueeze(2).to_broadcast([P, HEADS, DH])
            for m in range(MT):
                last = tt(by_head(xdt[:, m, :]), by_head(xtok[:, m, :]), spread(dts[:, 0, m, :]), ALU.mult)
            last.then_inc(xdt_ready, 1)
            for m in range(MT):
                link(tt(by_head(y[:, m, :]), by_head(xtok[:, m, :]), spread(heads4[:, 2, :]), ALU.mult))
            dve.wait_ge(sums_made, 1)
            copy(dts[:, 14, 0], banks[0][:, 32:48])
            copy(b_tok.rearrange("p g n -> p (g n)"), banks[0][:, P:P + 256])
            link(copy(dts[:, 6].rearrange("p m h -> p (m h)"), banks[0][:, 0:32]))
            tt(dts[:, 7, 0], dts[:, 14, 0], dts[:, 6, 0], ALU.subtract).then_inc(sums_ready, 1)
            dve.wait_ge(cb_made, 1)
            tt(cbm.rearrange("p m g l -> p (m g) l"), banks[1][:, :].rearrange("p (n l) -> p n l", n=4),
               upper[:, :].unsqueeze(1).to_broadcast([P, 4, P]), ALU.mult).then_inc(cb_ready, 1)
            turn(T_ATT)
            dve.wait_ge(end_exp, 1)
            dve.wait_ge(xdt_ready, 1)
            tt(by_head(xde), by_head(xdt[:, 0, :]), spread(dts[:, 9, 0]), ALU.mult).then_inc(xde_ready, 1)
            dve.wait_ge(cb_ready, 1)

            def segments(n):
                m, q = n // 4, n % 4
                dve.wait_ge(seg_made, n + 1)
                if m:
                    dve.wait_ge(diag_made, m)
                for h in range(4):
                    last = ts(decay[:, 4 * q + h, :], banks[n % 2][:, P * h:P * h + P], dts[:, 6, m, 4 * q + h:4 * q + h + 1],
                              0.0, ALU.subtract, ALU.min)
                last.then_inc(seg_ready, 1)

            def decays(n):
                m, q = n // 4, n % 4
                dve.wait_ge(decay_exp, n + 1)
                part = decay[:, 4 * q:4 * q + 4, :]
                tt(part, part, cbm[:, m, q // 2:q // 2 + 1, :].to_broadcast([P, 4, P]), ALU.mult).then_inc(decay_ready, 1)

            for m in range(MT):
                for q in range(4):
                    segments(4 * m + q)
                    if q:
                        decays(4 * m + q - 1)
                decays(4 * m + 3)
                dve.wait_ge(diag_made, m + 1)
                for half in range(2):
                    part = y[:, m, 512 * half:512 * half + 512]
                    last = tt(part, banks[2 + half][:, :], part, ALU.add)
                last.then_inc(diag_taken, 1)
            dve.wait_ge(off_made, 1)
            dve.wait_ge(diag_taken, 2)
            for half in range(2):
                hs = slice(8 * half, 8 * half + 8)
                link(tt(xde[:, 512 * half:512 * half + 512].rearrange("p (h d) -> p h d", h=8),
                            banks[2 + half][:, :].rearrange("p (h d) -> p h d", h=8),
                            dts[:, 8, 1, hs].unsqueeze(2).to_broadcast([P, 8, DH]), ALU.mult))
            link(tt(y[:, 1, :], y[:, 1, :], xde, ALU.add))
            dve.wait_ge(emptied_a, emptied("a", AT["z", 1]))
            for m in range(MT):
                last = tt(y[:, m, :], y[:, m, :], sz[:, m, :], ALU.mult)
            last.then_inc(y_gated, 1)
            dve.wait_ge(y_gated, 1)
            sum_squares(y, D // SSD_G, xtok, 2)
            rstd(4, D // SSD_G)
            for m in range(MT):
                for g in range(SSD_G):
                    part = y[:, m, 512 * g:512 * g + 512]
                    last = ts(part, part, stats[:, 8 + 2 * m + g:9 + 2 * m + g], None, ALU.mult)
            last.then_inc(y_gated, 1)
            turn(T_SSD)
            dve.wait_ge(panel_done, NP)
            dve.wait_ge(x_ready, X_OUT1)
            for b in range(4):
                part = x[:, b // 2, 512 * (b % 2):512 * (b % 2) + 512]
                tt(part, banks[4 + b][:, :], part, ALU.add).then_inc(x_ready, 1)
            norm_x(T_FFN2)
            turn(T_FFN2)
            dve.wait_ge(xn_d, 5)
            dve.wait_ge(xn_a, 5)
            dve.wait_ge(gains_loaded, 32)
            for m in range(MT):
                last = tt(t_rows[:, m, :], xn[:, m, :], gains[:, 0, :], ALU.mult)
            last.then_inc(t_ready, 1)
            dve.wait_ge(consts_made, 1)
            dve.wait_ge(routed, 1)
            link(copy(logits.rearrange("p m e -> p (m e)"), banks[0][:, 0:144]))
            eight = [P, MT, EG]

            by_group = one_hot[:, 5].rearrange("p m (g e) -> p m g e", g=EG)

            def first_of(values, at):
                top = rt[:, at + 1, :, 0:1]
                link(nc.vector.tensor_reduce(rt[:, at + 1, :, 0], values, AX_X, ALU.max))
                link(tt(rt[:, at + 2], values, top.to_broadcast(eight), ALU.is_lt))
                link(stt(rt[:, at + 2], rt[:, at + 2], 1000.0, iota[:, 0:EG].unsqueeze(1).to_broadcast(eight),
                         ALU.mult, ALU.add))
                link(nc.vector.tensor_reduce(rt[:, at + 3, :, 0], rt[:, at + 2], AX_X, ALU.min))
                link(tt(rt[:, at], iota[:, 0:EG].unsqueeze(1).to_broadcast(eight), rt[:, at + 3, :, 0:1].to_broadcast(eight),
                        ALU.is_equal))

            groups = logits[:, :, 0:EG]
            first_of(groups, 20)
            link(tt(rt[:, 2], groups, rt[:, 21, :, 0:1].to_broadcast(eight), ALU.subtract))
            link(tt(by_group, logits[:, :, EG:].rearrange("p m (g e) -> p m g e", g=EG),
                    rt[:, 20].unsqueeze(3).to_broadcast([P, MT, EG, EG]), ALU.mult))
            link(nc.vector.tensor_reduce(rt[:, 4], by_group.rearrange("p m g e -> p m e g"), AX_X, ALU.add))
            first_of(rt[:, 4], 24)
            link(stt(rt[:, 6], rt[:, 24], -3e38, rt[:, 4], ALU.mult, ALU.add))
            first_of(rt[:, 6], 28)
            tt(rt[:, 12, :, 0:1], rt[:, 29, :, 0:1], rt[:, 25, :, 0:1], ALU.subtract).then_inc(route_max, 1)
            dve.wait_ge(route_exp, 1)
            link(nc.vector.tensor_reduce(rt[:, 7, :, 0], rt[:, 3], AX_X, ALU.add))
            link(recip(rt[:, 8, :, 0:1], rt[:, 7, :, 0:1]))
            link(ts(rt[:, 9, :, 0:1], rt[:, 13, :, 0:1], 1.0, None, ALU.add))
            link(recip(rt[:, 10, :, 0:1], rt[:, 9, :, 0:1]))
            link(tt(rt[:, 10, :, 0:1], rt[:, 10, :, 0:1], rt[:, 8, :, 0:1], ALU.mult))
            link(tt(rt[:, 11, :, 0:1], rt[:, 10, :, 0:1], rt[:, 13, :, 0:1], ALU.mult))
            link(tt(rt[:, 14], rt[:, 24], rt[:, 28], ALU.add))
            link(tt(rt[:, 15], rt[:, 24], rt[:, 10, :, 0:1].to_broadcast(eight), ALU.mult))
            link(tt(rt[:, 16], rt[:, 28], rt[:, 11, :, 0:1].to_broadcast(eight), ALU.mult))
            link(tt(rt[:, 15], rt[:, 15], rt[:, 16], ALU.add))
            for n, values in ((2, rt[:, 14]), (3, rt[:, 15])):
                last = tt(one_hot[:, n].rearrange("p m (g e) -> p m g e", g=EG),
                          rt[:, 20].unsqueeze(3).to_broadcast([P, MT, EG, EG]),
                          values.unsqueeze(2).to_broadcast([P, MT, EG, EG]), ALU.mult)
            last.then_inc(marks_ready, 1)
            dve.wait_ge(ranks_made, 1)
            dve.wait_ge(marks_ready, 1)
            place = one_hot[:, 4]
            link(stt(place, banks[1][:, 0:2 * NE].rearrange("p (m e) -> p m e", m=MT), 1.0, one_hot[:, 2], ALU.add, ALU.mult))
            link(ts(place, place, -1.0, None, ALU.add))
            link(nc.vector.tensor_reduce(rt[:, 17, 0, 0:1], banks[1][:, 2 * NE:3 * NE], AX_X, ALU.max))
            copy(count_i[:, 0:NE], banks[1][:, 2 * NE:3 * NE])
            copy(count_i[:, NE:NE + 1], rt[:, 17, 0, 0:1]).then_inc(marks_done, 1)
            dve.wait_ge(marks_done, 1)
            dve.wait_ge(t_ready, 1)
            fullest = dve.value_load(count_i[0:1, NE:NE + 1], min_val=0, max_val=S)
            slots4 = iota[:, :].unsqueeze(1).unsqueeze(1).to_broadcast([P, MT, 2, SLOTS])

            def experts(i, pair, first):
                if not first:
                    dve.wait_ge(gathered, 2 * i)
                    dve.wait_ge(put_turned, i)
                at = bass.ds(pair * 2, 2)
                tt(pick, slots4, place[:, :, at].unsqueeze(3).to_broadcast([P, MT, 2, SLOTS]), ALU.is_equal).then_inc(picked, 1)
                dve.wait_ge(picked, i + 1)
                tt(pick_g, pick, one_hot[:, 3][:, :, at].unsqueeze(3).to_broadcast([P, MT, 2, SLOTS]), ALU.mult).then_inc(picked_g, 1)
                dve.wait_ge(gathered, 2 * i + 2)
                copy(xeT[:, 4:8, :].rearrange("p k s -> p (k s)"), banks[1][:, :]).then_inc(xe_d, 1)
                dve.wait_ge(silu_ready, i + 1)
                dve.wait_ge(upped, i + 1)
                tt(h_e, banks[3][:, :], h_e, ALU.mult).then_inc(he_ready, 1)
                dve.wait_ge(put_turned, i + 1)
                copy(put.rearrange("p m t -> p (m t)"), banks[1][:, 0:S]).then_inc(put_ready, 1)
                dve.wait_ge(downed, i + 1)
                copy(y_e[:, 512:1024], banks[3][:, :]).then_inc(ye_d, 1)

            experts(0, 0, True)
            with dve.Fori(1, PAIRS) as i:
                experts(i, i, False)
            with dve.If(fullest > SLOTS):
                for r in range(1, PASSES):
                    ts(place, place, -float(SLOTS), None, ALU.add).then_inc(moved, 1)
                    dve.wait_ge(moved, r)
                    with dve.Fori(0, PAIRS) as j:
                        experts(r * PAIRS + j, j, False)
            dve.wait_ge(y_summed, 1)
            for b in range(4):
                part = x[:, b // 2, 512 * (b % 2):512 * (b % 2) + 512]
                tt(part, banks[4 + b][:, :], part, ALU.add).then_inc(x_ready, 1)
            dve.wait_ge(x_ready, X_MOE)
            sum_squares(x, D, xn)
            rstd(MT, D)
            for m in range(MT):
                stt(xn[:, m, :], x[:, m, :], stats[:, 8 + m:9 + m], gains[:, 1, :], ALU.mult, ALU.mult).then_inc(out_ready, 1)


_INS = ['x', 'p', 'norm_mix_g', 'w_in', 'w_sgu_spatial', 'b_sgu_spatial', 'ln_v_g', 'ln_v_b', 'rel_bias', 'w_out',
        'norm_ffn_g', 'w_ff1', 'w_ff2', 'norm_ple_g', 'w_ple_gate', 'w_ple_proj', 'norm_final_g', 'norm_mix_2',
        'w_in_2', 'conv_w_2', 'conv_b_2', 'dt_bias_2', 'a_log_2', 'd_skip_2', 'ssd_norm_2', 'attn_sinks_2',
        'attn_norm_2', 'w_out_2', 'norm_ffn_2', 'w_router_group_2', 'w_router_expert_2', 'w_gate_2', 'w_up_2',
        'w_down_2', 'norm_final_2']


def bucket_line():
    distance = np.arange(LINE) - (P - 1)
    exact = BUCKETS // 2
    n = np.maximum(distance, exact)
    large = exact + np.floor(np.log(n / exact) / np.log(1024 / exact) * (BUCKETS - exact) + 1e-9).astype(int)
    bucket = np.where(distance < exact, distance, np.minimum(large, BUCKETS - 1))
    line = np.zeros((BUCKETS + 1, LINE), np.float32)
    line[np.maximum(bucket, 0), np.arange(LINE)] = distance >= 0
    line[BUCKETS, :P - 1] = MASKED
    return line


def kernel(**inputs):
    import concourse.bacc as _bacc
    from concourse.bass_utils import run_bass_kernel_spmd as _run

    nc = _bacc.Bacc("TRN2", target_bir_lowering=False, num_devices=1)
    arrays, args = {}, []
    given = [(name, np.ascontiguousarray(inputs[name])) for name in _INS] + [("bucket_line", bucket_line())]
    for name, a in given:
        arrays[f"in_{name}_dram"] = a
        args.append(nc.dram_tensor(f"in_{name}_dram", a.shape, mybir.dt.from_np(a.dtype), kind="ExternalInput").ap())
    out = nc.dram_tensor("out_0_dram", (1, S, D), F32, kind="ExternalOutput").ap()
    program(nc, *args, out)
    r = _run(nc, [arrays], core_ids=[0])
    return r.results[0]["out_0_dram"]
```

```python
from contextlib import ExitStack

import numpy as np

import concourse.bass as bass
from concourse import mybir

F32 = mybir.dt.float32
F32R = mybir.dt.float32r
I32 = mybir.dt.int32
ALU = mybir.AluOpType
ACT = mybir.ActivationFunctionType
AX_X = mybir.AxisListType.X

P = 128
D = 1024
S = 256
MT = S // P
KT = D // P
HEADS, DH = 16, 64
GROUPS = 8
BUCKETS = 32
D_FF = 4096
FT = D_FF // P
LINE = 512
SSD_G, SSD_N = 2, 128
CT = 12
TAPS = 4
NE, EG = 64, 8
FE = 512
SLOTS = 64
PAIRS = NE // 2
PASSES = S // SLOTS
EPS = 1e-6
MASKED = -1e30
RAW = 3
HALF = 2048
Q_SCALE = DH ** -0.5

PANELS = ([("v", 0), ("v", 1), ("u", 0), ("u", 1), ("q", 0), ("q", 1), ("k", 0), ("k", 1),
           ("va", 0), ("va", 1), ("gb", 0), ("gb", 1), ("ga", 0), ("ga", 1), ("wo", 0), ("wo", 1)]
          + [("ff1", j) for j in range(8)] + [("ff2", j) for j in range(8)]
          + [("pp", 0), ("pg", 0), ("pg", 1)]
          + [("q2", 0), ("q2", 1), ("kv2", 0), ("xbc", 0), ("xbc", 1), ("xbc", 2), ("z", 0), ("z", 1)]
          + [("wo2", 2), ("wo2", 3), ("wo2", 0), ("wo2", 1)])
NP = len(PANELS)
AT = {panel: p for p, panel in enumerate(PANELS)}
EMPTIED_BY = {"v": "aa", "u": "aa", "q": "ad", "k": "ad", "va": "ad", "gb": "aa", "ga": "aa", "wo": "dd",
              "ff1": "aa", "ff2": "", "pp": "", "pg": "aa", "q2": "ad", "kv2": "ad", "xbc": "ad",
              "z": "aa", "wo2": ""}
ROWS = {}
for _name, _n in (("norm_mix_g", 8), ("norm_ffn_g", 8), ("norm_ple_g", 8), ("b_sgu", 8), ("norm_mix_2", 8),
                  ("conv_w", TAPS * CT), ("conv_b", CT), ("ssd_norm", 8), ("attn_norm", 8), ("norm_ffn_2", 8)):
    ROWS[_name] = (sum(n for _, n in ROWS.values()), _n)
NROWS = sum(n for _, n in ROWS.values())


def emptied(engine, p):
    return sum(EMPTIED_BY[kind].count(engine) for kind, _ in PANELS[:p + 1])


def pair_of(p):
    return 2 * (sum(1 for kind, _ in PANELS[:p] if EMPTIED_BY[kind]) % 2)


def before_in_pair(p):
    users = [q for q in range(p) if EMPTIED_BY[PANELS[q][0]] and pair_of(q) == pair_of(p)]
    return users[-1] if users else None


def program(nc, x_in, p_in, norm_mix_g, w_in, w_sgu, b_sgu, ln_v_g, ln_v_b, rel_bias, w_out, norm_ffn_g,
            w_ff1, w_ff2, norm_ple_g, w_ple_gate, w_ple_proj, norm_final_g, norm_mix_2, w_in_2, conv_w,
            conv_b, dt_bias, a_log, d_skip, ssd_norm, attn_sinks, attn_norm, w_out_2, norm_ffn_2,
            w_router_group, w_router_expert, w_gate, w_up, w_down, norm_final, bucket_of_line, out):
    line_dram = nc.dram_tensor("bias_line", (HEADS, LINE), F32).ap()

    def columns(w, c0, n):
        return w[0, :, c0:c0 + n].rearrange("(k p) n -> p k n", p=P)

    def panel_source(kind, j):
        if kind in ("u", "v", "q", "k", "va", "ga", "gb"):
            at = ["u", "v", "q", "k", "va", "ga", "gb"].index(kind) * D
            return columns(w_in, at + 512 * j, 512)
        if kind in ("wo", "pg"):
            return columns({"wo": w_out, "pg": w_ple_gate}[kind], 512 * j, 512)
        if kind == "ff1":
            return columns(w_ff1, 512 * j, 512)
        if kind in ("ff2", "wo2"):
            w, rows, half = {"ff2": w_ff2, "wo2": w_out_2}[kind], D * (j // 2), 512 * (j % 2)
            return w[0, rows:rows + D, half:half + 512].rearrange("(k p) n -> p k n", p=P)
        if kind == "pp":
            return columns(w_ple_proj, 0, D)
        at = {"z": 0, "xbc": D, "q2": 2576, "kv2": 3600}[kind]
        return columns(w_in_2, at + 512 * j, 256 if kind == "kv2" else 512)

    with ExitStack() as ctx:
        def sb(name, shape, dt=F32):
            return ctx.enter_context(nc.sbuf_tensor(name, shape, dt))

        def sem(name):
            return ctx.enter_context(nc.semaphore(name))

        def in_turn(*phases):
            made = []
            for n, phase in enumerate(phases):
                with ExitStack() as place:
                    owner = ctx if n == len(phases) - 1 else place
                    made += [owner.enter_context(nc.sbuf_tensor(*one_of)) for one_of in phase]
            return made

        raw, w_hi, w_lo, h_lo, slots = in_turn(
            [("raw", [P, RAW, HALF], F32), ("w_hi", [P, 2, 2 * HALF], F32R), ("w_lo", [P, 2, 2 * HALF], F32R),
             ("h_lo", [P, KT, S], F32R)],
            [("slots", [P, 6, 4096], F32)])
        h_hi, hT = in_turn([("h_hi", [P, KT, S], F32R)], [("hT", [P, KT, S], F32)])
        hid_hi, hid_lo, areas = in_turn([("hid_hi", [P, FT, S], F32R), ("hid_lo", [P, FT, S], F32R)],
                                        [("areas", [P, 10, 2048], F32)])
        x = sb("x", [P, MT, D])
        soft = sb("soft", [P, 2, 384])
        softT = sb("softT", [P, 2, 384])
        cols = sb("cols", [P, NROWS])
        ident = sb("ident", [P, P])
        upper = sb("upper", [P, P])
        above = sb("above", [P, P])
        ones = sb("ones", [P, P])
        one = sb("one", [P, 2])
        window = sb("window", [P, S])
        table = sb("table", [BUCKETS + 1, HEADS])
        stats = sb("stats", [P, 16])
        peak = sb("peak", [P, 4, 2])
        head_sum = sb("head_sum", [P, 4, 4])
        sink_e = sb("sink_e", [P, 4, 2])
        heads4 = sb("heads4", [P, 4, HEADS])
        neg_sink = sb("neg_sink", [P, HEADS])
        dtw_hi, dtw_lo = sb("dtw_hi", [P, KT, HEADS], F32R), sb("dtw_lo", [P, KT, HEADS], F32R)
        dts_all = sb("dts_all", [P, 16 * MT * HEADS])
        dtw = dts_all[:, 0:KT * HEADS].rearrange("p (k h) -> p k h", k=KT)
        iota = sb("iota", [P, SLOTS])
        count_i = sb("count_i", [P, NE + 1], I32)
        iota_i = count_i[:, 0:SLOTS]

        def area(n, k=1):
            return areas[:, n:n + k, :].rearrange("p a n -> p (a n)")

        def rows_area(n):
            return area(n).rearrange("p (m c) -> p m c", m=MT)

        def cols_area(n, tiles=KT):
            return area(n, tiles * S // 2048).rearrange("p (k t) -> p k t", k=tiles)

        xn = rows_area(9)
        v_rows, u_rows, qT, kT, va, sga, sgb, yb = (rows_area(0), rows_area(1), cols_area(2), cols_area(3),
                                                   rows_area(4), rows_area(5), rows_area(6), rows_area(9))
        bias = area(7, 2).rearrange("p (h j) -> p h j", h=HEADS)
        w_s = area(7)[:, 0:1024].rearrange("p (g s) -> p g s", g=GROUPS)
        w_sT = area(7)[:, 1024:2048].rearrange("p (g s) -> p g s", g=GROUPS)
        small_rows = area(5)[0:NROWS, 0:P]
        ln_vecs = rows_area(4)
        hid = area(9)
        final_g = area(8)[:, 0:D]
        xg = rows_area(7)
        p_rows = area(8)[:, 1024:1536].rearrange("p (m c) -> p m c", m=MT)
        pT_hi, pT_lo = h_hi[:, 0:2, :], h_lo[:, 0:2, :]
        gate_rows = rows_area(5)
        q2T, xraw, xc, sz = (cols_area(0), area(1, 2)[:, 0:CT * (S + TAPS - 1)].rearrange("p (c t) -> p c t", c=CT),
                             area(3, 2)[:, 0:CT * S].rearrange("p (c t) -> p c t", c=CT), rows_area(5))
        xtok, xdt, y, att = rows_area(6), rows_area(7), rows_area(8), rows_area(9)
        k2T = area(4)[:, 1024:1536].rearrange("p (g t) -> p g t", g=2)
        v2 = area(4)[:, 1536:1792].rearrange("p (m c) -> p m c", m=MT)
        b_tok = area(4)[:, 1792:2048].rearrange("p (g n) -> p g n", g=2)
        dt_cols = area(3)[0:HEADS, 0:S]
        decay = area(1).rearrange("p (h l) -> p h l", h=HEADS)
        state = area(2)[:, 0:1024]
        xde = area(2)[:, 1024:2048]
        cbm = sb("cbm_all", [P, 512])[:, :].rearrange("p (m g l) -> p m g l", m=MT, g=2)
        dts = dts_all[:, :].rearrange("p (n m h) -> p n m h", n=16, m=MT)
        t_rows = rows_area(0)
        zeros = area(4)[:, 0:256].bitcast(mybir.dt.bfloat16)
        gains = rows_area(5)
        routerw = area(4)[:, 512:512 + KT * (EG + NE)].rearrange("p (k n) -> p k n", k=KT)
        xeT = area(1)[:, 0:1024].rearrange("p (k s) -> p k s", k=KT)
        h_e = area(1)[:, 1024:1536]
        heT = area(1)[:, 1536:2048].rearrange("p (c s) -> p c s", c=4)
        y_e = area(2)[:, 0:1024]
        pick = area(2)[:, 1024:1280].rearrange("p (m e s) -> p m e s", m=MT, e=2)
        pick_g = area(2)[:, 1280:1536].rearrange("p (m e s) -> p m e s", m=MT, e=2)
        put = area(2)[:, 1536:1792].rearrange("p (m t) -> p m t", m=MT)
        logits = area(3)[:, 0:144].rearrange("p (m e) -> p m e", m=MT)
        rt = area(3)[:, 144:144 + 56 * 16].rearrange("p (n m e) -> p n m e", n=56, m=MT)
        one_hot = area(3)[:, 1100:1100 + 768].rearrange("p (n m e) -> p n m e", n=6, m=MT)

        banks = [ctx.enter_context(nc.psum_tensor(f"bank{b}", [P, 512], F32)) for b in range(8)]

        x_loaded, p_loaded, rows_loaded, ws_loaded = sem("x_loaded"), sem("p_loaded"), sem("rows_loaded"), sem("ws_loaded")
        ln_loaded, table_loaded, bucket_loaded, heads_loaded = (sem("ln_loaded"), sem("table_loaded"),
                                                                sem("bucket_loaded"), sem("heads_loaded"))
        dtw_loaded, router_loaded, line_stored, bias_loaded = (sem("dtw_loaded"), sem("router_loaded"),
                                                               sem("line_stored"), sem("bias_loaded"))
        gains_loaded, out_stored = sem("gains_loaded"), sem("out_stored")
        landed = [sem(f"half_landed{s}") for s in range(RAW)]
        w_rounded, w_ready = sem("w_rounded"), sem("w_ready")
        panel_done, emptied_a, emptied_d = sem("panel_done"), sem("emptied_by_scalar"), sem("emptied_by_vector")
        consts_made, ws_masked = sem("consts_made"), sem("ws_masked")
        act_step, dve_step, pool_step = sem("act_step"), sem("dve_step"), sem("pool_step")
        rows_turned, cols_ready, ws_turned, wsT_ready = (sem("rows_turned"), sem("cols_ready"), sem("ws_turned"),
                                                         sem("wsT_ready"))
        line_ready, line_copied, p_turned, pT_ready = sem("line_ready"), sem("line_copied"), sem("p_turned"), sem("pT_ready")
        squares, mean_ready, root_ready, rstd_ready = sem("squares"), sem("mean_ready"), sem("root_ready"), sem("rstd_ready")
        xn_a, xn_d, turned, hT_a, hT_d = sem("xn_by_scalar"), sem("xn_by_vector"), sem("turned"), sem("hT_by_scalar"), sem("hT_by_vector")
        v_mean, v_root, v_normed = sem("v_mean"), sem("v_root"), sem("v_normed")
        xg_ready = sem("xg_ready")
        table_ones, final_loaded, zeros_made, picked_g, moved = (sem("table_ones"), sem("final_loaded"), sem("zeros_made"),
                                                                 sem("picked_g"), sem("moved"))
        sgu_mixed, ya_ready = sem("sgu_mixed"), sem("ya_ready")
        scored, scores_taken, peak_ready, probs_ready = sem("scored"), sem("scores_taken"), sem("peak_ready"), sem("probs_ready")
        probs_turned, softT_ready, heads_out, heads_kept = sem("probs_turned"), sem("softT_ready"), sem("heads_out"), sem("heads_kept")
        merged, x_ready, hid_squared, hid_rounded, hid_ready = (sem("merged"), sem("x_ready"), sem("hid_squared"),
                                                                sem("hid_rounded"), sem("hid_ready"))
        pT_rounded = sem("pT_rounded")
        sink_ready = sem("sink_ready")
        dtw_rounded, dtw_ready, dt_kept, dt_turned = sem("dtw_rounded"), sem("dtw_ready"), sem("dt_kept"), sem("dt_turned")
        dt_made, dt_in, dt_exp, dt_log, dt_ready = sem("dt_made"), sem("dt_in"), sem("dt_exp"), sem("dt_log"), sem("dt_ready")
        w_exp, conv_ready, xc_ready, pads_zero = sem("w_exp"), sem("conv_ready"), sem("xc_ready"), sem("pads_zero")
        x_turned, xtok_a, xtok_d, xdt_ready = sem("x_turned"), sem("xtok_by_scalar"), sem("xtok_by_vector"), sem("xdt_ready")
        sums_made, sums_ready, cb_made, cb_ready = sem("sums_made"), sem("sums_ready"), sem("cb_made"), sem("cb_ready")
        end_exp, seg_made, seg_ready, decay_exp, decay_ready = sem("end_exp"), sem("seg_made"), sem("seg_ready"), sem("decay_exp"), sem("decay_ready")
        diag_made, diag_taken, xde_ready, state_made, state_ready, off_made = (sem("diag_made"), sem("diag_taken"), sem("xde_ready"),
                                                                               sem("state_made"), sem("state_ready"), sem("off_made"))
        y_gated, att_ready = sem("y_gated"), sem("att_ready")
        t_ready, routed, route_max, route_exp, marks_ready, ranks_made, marks_done = (
            sem("t_ready"), sem("routed"), sem("route_max"), sem("route_exp"), sem("marks_ready"), sem("ranks_made"), sem("marks_done"))
        pair_landed = {(w, e): sem(f"{w}{e}_landed") for w in ("gate", "odd_gate", "up", "down")
                       for e in range(2)}
        picked, gathered, xe_a, xe_d = sem("picked"), sem("gathered"), sem("xe_by_scalar"), sem("xe_by_vector")
        gated, upped, silu_ready, he_ready = sem("gated"), sem("upped"), sem("silu_ready"), sem("he_ready")
        he_turned, heT_ready, put_turned, put_ready = sem("he_turned"), sem("heT_ready"), sem("put_turned"), sem("put_ready")
        downed, ye_a, ye_d, scattered, y_summed = sem("downed"), sem("ye_by_scalar"), sem("ye_by_vector"), sem("scattered"), sem("y_summed")
        out_ready = sem("out_ready")

        def col(name, k):
            return cols[:, ROWS[name][0] + k:ROWS[name][0] + k + 1]

        def linker(eng, step):
            count = [0]

            def link(ins):
                count[0] += 1
                ins.then_inc(step, 1)
                eng.wait_ge(step, count[0])
            return link

        def shape(p):
            return {"pp": (2, 1024), "kv2": (8, 256)}.get(PANELS[p][0], (8, 512))

        def loaded(q):
            k, n = shape(q // 2)
            return raw[:, q % RAW, 0:k * n // 2].rearrange("p (k n) -> p k n", n=n)

        def pieces(q):
            at = shape(q // 2)[0] // 2
            source, (hi, lo) = loaded(q), [w[:, at * (q % 2):at * (q % 2) + at, :] for w in parts(q // 2)]
            if PANELS[q // 2][0] != "kv2":
                return [(source, hi, lo)]
            twice = lambda w, g: w[:, :, P * g:P * g + P].rearrange("p k (two d) -> p k two d", two=2)
            return [(source[:, :, DH * g:DH * g + DH].unsqueeze(2).to_broadcast([P, at, 2, DH]), twice(hi, g), twice(lo, g))
                    for g in range(2)] + [(source[:, :, P:], hi[:, :, 2 * P:], lo[:, :, 2 * P:])]

        def parts(p):
            k, n = shape(p)
            n += P if PANELS[p][0] == "kv2" else 0
            return [w[:, p % 2, 0:k * n].rearrange("p (k n) -> p k n", k=k) for w in (w_hi, w_lo)]

        def expert_panel(w, e, odd):
            s = {"gate": 0, "up": 2, "down": 4}[w] + e
            place = area(6 + 2 * e, 2) if w == "gate" and odd else slots[:, s, :]
            return place.rearrange("p (k n) -> p k n", k=4 if w == "down" else 8)

        TURNS = [(xn, "norm_mix_g"), (yb, None), (xn, "norm_ffn_g"), (xn, "norm_ple_g"),
                 (xn, "norm_mix_2"), (att, "attn_norm"), (y, "ssd_norm"), (xn, "norm_ffn_2")]
        T_MIX, T_MERGED, T_FFN, T_PLE, T_MIX2, T_ATT, T_SSD, T_FFN2 = range(8)
        X_MLP, X_PLE, X_OUT1, X_MIX2, X_MOE = 4, 8, 10, 14, 18
        SPLIT_AT = (0, 1, 4, 5, 8, 9, 12, 13)
        NORM_OF = {T_MIX: 0, T_FFN: 1, T_PLE: 2, T_MIX2: 3, T_FFN2: 4}

        block = ctx.enter_context(nc.Block())

        @block.sync
        def _(sp):
            sp.dma_start(x[:, :, :], x_in[0].rearrange("(m p) c -> p m c", p=P)).then_inc(x_loaded, 16)
            def load_rows():
                sources = {"norm_mix_g": norm_mix_g, "norm_ffn_g": norm_ffn_g, "norm_ple_g": norm_ple_g, "b_sgu": b_sgu,
                           "norm_mix_2": norm_mix_2, "conv_w": conv_w, "conv_b": conv_b, "ssd_norm": ssd_norm,
                           "attn_norm": attn_norm, "norm_ffn_2": norm_ffn_2}
                for name, (first, n) in ROWS.items():
                    src = sources[name]
                    if name == "conv_w":
                        src = src[0].rearrange("j (c p) -> (j c) p", p=P)
                    elif name == "b_sgu":
                        src = src[0]
                    else:
                        src = src[0].rearrange("(c p) -> c p", p=P)
                    sp.dma_start(small_rows[first:first + n], src).then_inc(rows_loaded, 16)

            for q in range(2 * NP):
                p, (kind, j) = q // 2, PANELS[q // 2]
                k = shape(p)[0] // 2
                if q >= RAW:
                    sp.wait_ge(w_ready, q - RAW + 1)
                sp.dma_start(loaded(q),
                             panel_source(kind, j)[:, k * (q % 2):k * (q % 2) + k, :]).then_inc(landed[q % RAW], 16)
                if q == 0:
                    load_rows()
                if q == 1:
                    sp.dma_start(table[0:BUCKETS, :], rel_bias).then_inc(table_loaded, 16)
                    sp.dma_start(area(6)[0:BUCKETS + 1, 0:LINE], bucket_of_line).then_inc(bucket_loaded, 16)
                    sp.dma_start(w_s, w_sgu[0].rearrange("g t s -> t g s")).then_inc(ws_loaded, 16)
                if q == 3:
                    sp.dma_start(ln_vecs[:, 0, :], ln_v_g.to_broadcast([P, D])).then_inc(ln_loaded, 16)
                    sp.dma_start(ln_vecs[:, 1, :], ln_v_b.to_broadcast([P, D])).then_inc(ln_loaded, 16)
                if q == 11:
                    for n, v in enumerate((dt_bias, a_log, d_skip, attn_sinks)):
                        sp.dma_start(heads4[:, n, :], v.to_broadcast([P, HEADS])).then_inc(heads_loaded, 16)
                    sp.dma_start(dtw[:, :, :], columns(w_in_2, 2560, HEADS)).then_inc(dtw_loaded, 16)
            def load(w, i, pair, odd, beyond):
                weights, used = {"gate": (w_gate, gated), "up": (w_up, upped), "down": (w_down, downed)}[w]
                tokens = [None if beyond is None else tokens_of(pair, e) for e in range(2)]
                if isinstance(i, int) and i == 0:
                    sp.wait_ge(panel_done, NP)
                elif isinstance(i, int) and w == "gate":
                    sp.wait_ge(t_ready, 1)
                    sp.wait_ge(routed, 1)
                else:
                    sp.wait_ge(used, i - 1 if w == "gate" else i)
                for e in range(2):
                    cond = {} if beyond is None else {"cond": tokens[e] > beyond}
                    sp.dma_start(expert_panel(w, e, odd), weights[0, 2 * pair + e].rearrange("(k p) n -> p k n", p=P),
                                 **cond).then_inc(pair_landed["odd_gate" if w == "gate" and odd else w, e], 16)

            def tokens_of(pair, e):
                return sp.value_load(count_i[0:1, bass.ds(2 * pair + e, 1)], min_val=0, max_val=S)

            def rest_of_pass(first, beyond):
                with sp.Fori(0, PAIRS // 2 - 1) as j:
                    for n in (1, 2):
                        for w, ahead in (("up", 0), ("down", 0), ("gate", 1)):
                            load(w, 2 * j + n + ahead + first, 2 * j + n + ahead, (n + ahead) % 2, beyond)
                for w in ("up", "down"):
                    load(w, first + PAIRS - 1, PAIRS - 1, 1, beyond)

            for w in ("gate", "up", "down"):
                load(w, 0, 0, 0, None)
            load("gate", 1, 1, 1, None)
            sp.wait_ge(marks_done, 1)
            fullest = sp.value_load(count_i[0:1, NE:NE + 1], min_val=0, max_val=S)
            rest_of_pass(0, 0)
            with sp.If(fullest > SLOTS):
                with sp.Fori(1, PASSES) as r:
                    for w in ("gate", "up", "down"):
                        load(w, r * PAIRS, 0, 0, r * SLOTS)
                    load("gate", r * PAIRS + 1, 1, 1, r * SLOTS)
                    rest_of_pass(r * PAIRS, r * SLOTS)
            for m in range(MT):
                sp.wait_ge(out_ready, m + 1)
                sp.dma_start(out[0, P * m:P * m + P, :], xn[:, m, :]).then_inc(out_stored, 16)
            sp.wait_ge(out_stored, 16 * MT)

        @block.gpsimd
        def _(pool):
            link = linker(pool, pool_step)
            for made in (ident[:, :], window[:, :]):
                nc.gpsimd.memset(made, 0.0)
            for made in (upper[:, :], above[:, :], one[:, :], ones[:, :]):
                link(nc.gpsimd.memset(made, 1.0))
            nc.gpsimd.affine_select(out=ident[:, :], in_=ident[:, :], compare_op=ALU.not_equal, fill=1.0, base=0,
                                    pattern=[[-1, P]], channel_multiplier=1)
            nc.gpsimd.affine_select(out=upper[:, :], in_=upper[:, :], compare_op=ALU.is_ge, fill=0.0, base=0,
                                    pattern=[[1, P]], channel_multiplier=-1)
            nc.gpsimd.affine_select(out=above[:, :], in_=above[:, :], compare_op=ALU.is_gt, fill=0.0, base=0,
                                    pattern=[[1, P]], channel_multiplier=-1)
            link(nc.gpsimd.affine_select(out=window[:, :], in_=window[:, :], compare_op=ALU.is_gt, fill=MASKED, base=0,
                                         pattern=[[1, S]], channel_multiplier=-1))
            nc.gpsimd.affine_select(out=window[:, :], in_=window[:, :], compare_op=ALU.is_ge, fill=MASKED, base=P,
                                    pattern=[[-1, S]], channel_multiplier=1)
            link(nc.gpsimd.iota(iota_i, pattern=[[1, SLOTS]], base=0, channel_multiplier=0))
            nc.gpsimd.tensor_copy(iota[:, :], iota_i).then_inc(consts_made, 1)
            pool.wait_ge(ws_loaded, 16)
            nc.gpsimd.affine_select(out=w_s, in_=w_s, compare_op=ALU.is_ge, fill=0.0, base=0,
                                    pattern=[[0, GROUPS], [-1, P]], channel_multiplier=1).then_inc(ws_masked, 1)
            pool.wait_ge(line_copied, 1)
            pool.dma_start(line_dram, soft[0:HEADS, :, :].rearrange("p a b -> p (a b)")[:, 0:LINE]).then_inc(line_stored, 16)
            pool.wait_ge(line_stored, 16)
            pool.wait_ge(sgu_mixed, 4)
            pool.dma_start(bias, bass.AP(line_dram.tensor, 0, [[1, P], [LINE, HEADS], [1, S]])).then_inc(bias_loaded, 16)
            pool.wait_ge(merged, MT)
            pool.dma_start(final_g, norm_final_g.rearrange("(a n) -> a n", a=1).to_broadcast([P, D])).then_inc(final_loaded, 16)
            pool.dma_start(p_rows, p_in[0, 0].rearrange("(m p) c -> p m c", p=P)).then_inc(p_loaded, 16)
            pool.wait_ge(rstd_ready, 5)
            for m in range(MT):
                nc.gpsimd.tensor_scalar(x[:, m, :], xg[:, m, :], stats[:, 8 + m:9 + m], 1.0, ALU.mult, ALU.mult).then_inc(x_ready, 1)
            nc.gpsimd.memset(xraw[:, :, 0:TAPS - 1], 0.0).then_inc(pads_zero, 1)
            pool.wait_ge(y_gated, 1)
            pool.dma_start(gains[:, 0, :], norm_ffn_2.to_broadcast([P, D])).then_inc(gains_loaded, 16)
            pool.dma_start(gains[:, 1, :], norm_final.rearrange("(a n) -> a n", a=1).to_broadcast([P, D])).then_inc(gains_loaded, 16)
            pool.dma_start(routerw[:, :, 0:EG], columns(w_router_group, 0, EG)).then_inc(router_loaded, 16)
            pool.dma_start(routerw[:, :, EG:], columns(w_router_expert, 0, NE)).then_inc(router_loaded, 16)
            nc.gpsimd.memset(area(4)[:, 0:256], 0.0).then_inc(zeros_made, 1)

        @block.scalar
        def _(act):
            link = linker(act, act_step)
            act_ = nc.scalar.activation
            def sum_squares(src, n, squared, first=0):
                for i in range(D // n):
                    part = slice(n * i, n * i + n)
                    last = act_(squared[:, 0, part], src[:, 0, part], ACT.Square,
                                accum_out=stats[:, first + i:first + i + 1])
                last.then_inc(squares, 1)

            def load_roots():
                act_(one[:, 1:2], one[:, 0:1], ACT.Sqrt)

            norms = [0]

            def norm(t, n_stats):
                norms[0] += 1
                act.wait_ge(mean_ready, norms[0])
                act_(stats[:, 4:4 + n_stats], stats[:, 4:4 + n_stats], ACT.Sqrt).then_inc(root_ready, 1)

            def norm_x(t):
                load_roots()
                if t == T_MIX:
                    act.wait_ge(x_loaded, 16)
                elif t == T_FFN:
                    act.wait_ge(emptied_d, emptied("d", AT["wo", 1]))
                else:
                    act.wait_ge(x_ready, {T_PLE: X_MLP, T_MIX2: X_OUT1, T_FFN2: X_MIX2}[t])
                sum_squares(x, D, xn)
                norm(t, MT)
                act.wait_ge(rstd_ready, norms[0])
                act_(xn[:, 1, :], x[:, 1, :], ACT.Copy, scale=stats[:, 9:10]).then_inc(xn_a, 1)

            def turn(t):
                _, gain = TURNS[t]
                for b in (1, 3) if t == T_FFN2 else range(4):
                    act.wait_ge(turned, 4 * t + b + 1)
                    for k in (2 * b, 2 * b + 1):
                        psum = banks[b][:, S * (k % 2):S * (k % 2) + S]
                        last = act_((hT if t == T_FFN2 else h_hi)[:, k, :], psum, ACT.Copy, scale=col(gain, k) if gain else 1.0)
                    last.then_inc(hT_a, 1)

            def split(*halves):
                for q in halves:
                    act.wait_ge(landed[q % RAW], 16 * (q // RAW + 1))
                    if q >= 4:
                        act.wait_ge(panel_done, q // 2 - 1)
                    for source, hi, _ in pieces(q):
                        last = act_(hi, source, ACT.Copy)
                    last.then_inc(w_rounded, 1)

            def split_panel(p):
                split(2 * p, 2 * p + 1)

            def empty(kind, j):
                p = AT[kind, j]
                act.wait_ge(panel_done, p + 1)
                for b, engine in enumerate(EMPTIED_BY[kind]):
                    if engine != "a":
                        continue
                    bank = banks[pair_of(p) + b]
                    half = slice(512 * j, 512 * j + 512)
                    if kind in ("v", "u"):
                        ins = act_((v_rows if kind == "v" else u_rows)[:, b, half], bank[:, :], ACT.Gelu_apprx_tanh)
                    elif kind in ("ga", "gb", "pg"):
                        ins = act_({"ga": sga, "gb": sgb, "pg": gate_rows}[kind][:, b, half], bank[:, :], ACT.Sigmoid)
                    elif kind == "z":
                        ins = act_(sz[:, b, half], bank[:, :], ACT.Silu)
                    elif kind in ("q", "k", "q2"):
                        dst = {"q": qT, "k": kT, "q2": q2T}[kind][:, 4 * j + 2 * b:4 * j + 2 * b + 2, :]
                        ins = act_(dst.rearrange("p k t -> p (k t)"), bank[:, :], ACT.Copy,
                                   scale=1.0 if kind == "k" else Q_SCALE)
                    elif kind == "va":
                        ins = act_(va[:, b, half], bank[:, :], ACT.Copy)
                    elif kind == "ff1":
                        if j >= 2:
                            act.wait_ge(hid_ready, 2 * (j - 2) + b + 1)
                        ins = act_(hid[:, 1024 * (j % 2) + 512 * b:1024 * (j % 2) + 512 * b + 512], bank[:, :], ACT.Relu)
                    elif kind == "kv2":
                        ins = act_(k2T.rearrange("p g t -> p (g t)"), bank[:, :], ACT.Copy)
                    elif kind == "xbc":
                        ins = act_(xraw[:, 4 * j + 2 * b:4 * j + 2 * b + 2, TAPS - 1:],
                                   bank[:, :].rearrange("p (c t) -> p c t", c=2), ACT.Copy)
                    ins.then_inc(emptied_a, 1)

            def hidden(j):
                for b in range(2):
                    act.wait_ge(hid_squared, 2 * j + b + 1)
                    at = 1024 * (j % 2) + 512 * b
                    act_(hid_hi[:, 4 * j + 2 * b:4 * j + 2 * b + 2, :].rearrange("p k t -> p (k t)"), hid[:, at:at + 512],
                         ACT.Copy).then_inc(hid_rounded, 1)

            def head_exp(n):
                b = n % 2
                act.wait_ge(peak_ready, n + 1)
                act_(soft[:, b, 0:S], soft[:, b, 0:S], ACT.Exp, bias=peak[:, n % 4, 0:1], accum_out=head_sum[:, n % 4, 0:1])
                last = act_(soft[:, b, S:], soft[:, b, S:], ACT.Exp, bias=peak[:, n % 4, 1:2], accum_out=head_sum[:, n % 4, 1:2])
                if n >= HEADS:
                    last = act_(sink_e[:, n % 4, :], peak[:, n % 4, 0:2], ACT.Exp, bias=heads4[:, 3, n - HEADS:n - HEADS + 1])
                last.then_inc(probs_ready, 1)

            def head_turned(n):
                act.wait_ge(probs_turned, n + 1)
                if n >= 2:
                    act.wait_ge(heads_out, n - 1)
                act_(softT[:, n % 2, :], banks[6 + n % 2][:, 0:384], ACT.Copy).then_inc(softT_ready, 1)

            act.wait_ge(consts_made, 1)
            norm_x(T_MIX)
            split(0)
            act.wait_ge(cols_ready, 1)
            turn(T_MIX)
            split(1)
            split_panel(1)
            for kind, j in (("v", 0), ("v", 1), ("u", 0)):
                empty(kind, j)
                split_panel(AT[kind, j] + 2)
            act.wait_ge(v_mean, 1)
            act_(stats[:, 14:16], stats[:, 14:16], ACT.Sqrt).then_inc(v_root, 1)
            for kind, j in (("u", 1), ("q", 0), ("q", 1), ("k", 0), ("k", 1), ("va", 0), ("va", 1)):
                empty(kind, j)
                if (kind, j) != ("va", 1):
                    split_panel(AT[kind, j] + 2)
            for step in range(HEADS + 2):
                if step < HEADS:
                    head_exp(step)
                if 1 <= step <= HEADS:
                    head_turned(step - 1)
                if step < HEADS and step % 4 == 3:
                    empty(("gb", "ga")[step // 8], (step // 4) % 2)
                if step in SPLIT_AT:
                    split(2 * AT["gb", 1] + SPLIT_AT.index(step))
            turn(T_MERGED)
            split_panel(AT["wo", 1])
            split_panel(AT["ff1", 0])
            norm_x(T_FFN)
            turn(T_FFN)
            split_panel(AT["ff1", 1])
            for j in range(8):
                empty("ff1", j)
                split_panel(AT["ff1", j] + 2)
                hidden(j)
            act.wait_ge(p_turned, 1)
            act_(pT_hi.rearrange("p k t -> p (k t)"), banks[0][:, :], ACT.Copy).then_inc(pT_rounded, 1)
            for p in range(AT["ff2", 2], AT["pg", 0]):
                split_panel(p)
            norm_x(T_PLE)
            split(2 * AT["pg", 0])
            turn(T_PLE)
            split(2 * AT["pg", 0] + 1)
            split_panel(AT["pg", 1])
            act.wait_ge(dtw_loaded, 16)
            act_(dtw_hi[:, :, :], dtw[:, :, :], ACT.Copy).then_inc(dtw_rounded, 1)
            for j in range(2):
                empty("pg", j)
                if j == 0:
                    split_panel(AT["q2", 0])
            load_roots()
            act.wait_ge(x_ready, X_PLE)
            sum_squares(x, D, rows_area(3))
            act.wait_ge(xg_ready, 2)
            sum_squares(xg, D, rows_area(2), 2)
            norms[0] += 2
            act.wait_ge(mean_ready, norms[0])
            act_(stats[:, 4:8], stats[:, 4:8], ACT.Sqrt).then_inc(root_ready, 2)
            act.wait_ge(rstd_ready, norms[0])
            act_(xn[:, 1, :], xg[:, 1, :], ACT.Copy, scale=stats[:, 11:12]).then_inc(xn_a, 1)
            turn(T_MIX2)
            split_panel(AT["q2", 1])
            for kind, j in (("q2", 0), ("q2", 1), ("kv2", 0)):
                empty(kind, j)
                if kind == "q2":
                    split_panel(AT[kind, j] + 2)
            act.wait_ge(dt_in, 1)
            act_(dts[:, 2], dts[:, 1], ACT.Exp, scale=-1.0).then_inc(dt_exp, 1)
            act.wait_ge(heads_loaded, 64)
            act_(heads4[:, 1, :], heads4[:, 1, :], ACT.Exp).then_inc(w_exp, 1)
            act.wait_ge(dt_in, 2)
            act_(dts[:, 4], dts[:, 3], ACT.Ln).then_inc(dt_log, 1)
            for step in range(HEADS + 2):
                if step < HEADS:
                    head_exp(HEADS + step)
                if 1 <= step <= HEADS:
                    head_turned(HEADS + step - 1)
                if step % 4 == 3 and step < HEADS:
                    empty(*(("xbc", 0), ("xbc", 1), ("xbc", 2), ("z", 0))[step // 4])
                if step in SPLIT_AT:
                    split(2 * AT["xbc", 1] + SPLIT_AT.index(step))
            split_panel(AT["wo2", 2])
            for j in range(3):
                act.wait_ge(conv_ready, 4 * j + 4)
                part = xc[:, 4 * j:4 * j + 4, :].rearrange("p c t -> p (c t)")
                act_(part, part, ACT.Silu).then_inc(xc_ready, 1)
            load_roots()
            act.wait_ge(heads_kept, 2 * HEADS)
            sum_squares(att, D, rows_area(0))
            norm(T_ATT, MT)
            empty("z", 1)
            for b in (1, 3):
                act.wait_ge(x_turned, b + 1)
                act_(xtok[:, b // 2, 512:1024], banks[b][:, :], ACT.Copy).then_inc(xtok_a, 1)
            act.wait_ge(sums_ready, 1)
            act_(dts[:, 8], dts[:, 6], ACT.Exp)
            act_(dts[:, 9, 0], dts[:, 7, 0], ACT.Exp).then_inc(end_exp, 1)
            turn(T_ATT)
            split_panel(AT["wo2", 3])
            for n in range(8):
                act.wait_ge(seg_ready, n + 1)
                part = decay[:, 4 * (n % 4):4 * (n % 4) + 4, :].rearrange("p h l -> p (h l)")
                act_(part, part, ACT.Exp).then_inc(decay_exp, 1)
            act.wait_ge(state_made, 1)
            act_(state[:, 0:512], banks[0][:, :], ACT.Copy)
            act_(state[:, 512:1024], banks[1][:, :], ACT.Copy).then_inc(state_ready, 1)
            split_panel(AT["wo2", 0])
            load_roots()
            act.wait_ge(y_gated, 1)
            sum_squares(y, D // SSD_G, xtok)
            norm(T_SSD, 4)
            turn(T_SSD)
            split_panel(AT["wo2", 1])
            norm_x(T_FFN2)
            turn(T_FFN2)
            act.wait_ge(route_max, 1)
            act_(rt[:, 3], rt[:, 2], ACT.Exp)
            act_(rt[:, 13, :, 0:1], rt[:, 12, :, 0:1], ACT.Exp).then_inc(route_exp, 1)
            act.wait_ge(marks_done, 1)
            fullest = act.value_load(count_i[0:1, NE:NE + 1], min_val=0, max_val=S)

            def gather(i):
                act.wait_ge(gathered, 2 * i + 1)
                act_(xeT[:, 0:4, :].rearrange("p k s -> p (k s)"), banks[0][:, :], ACT.Copy).then_inc(xe_a, 1)

            def experts(i, last=False):
                act.wait_ge(gated, i + 1)
                act_(h_e, banks[2][:, :], ACT.Silu).then_inc(silu_ready, 1)
                act.wait_ge(he_turned, i + 1)
                act_(heT.rearrange("p c s -> p (c s)"), banks[0][:, :], ACT.Copy).then_inc(heT_ready, 1)
                if not last:
                    gather(i + 1)
                act.wait_ge(downed, i + 1)
                act_(y_e[:, 0:512], banks[2][:, :], ACT.Copy).then_inc(ye_a, 1)

            gather(0)
            with act.Fori(0, PAIRS - 1) as i:
                experts(i)
            experts(PAIRS - 1, True)
            with act.If(fullest > SLOTS):
                with act.Fori(1, PASSES) as r:
                    gather(r * PAIRS)
                    with act.Fori(0, PAIRS - 1) as j:
                        experts(r * PAIRS + j)
                    experts(r * PAIRS + (PAIRS - 1), True)
            load_roots()
            act.wait_ge(x_ready, X_MOE)
            sum_squares(x, D, xn)
            norm(None, MT)

        @block.tensor
        def _(pe):
            mm, turn_tile = nc.tensor.matmul, nc.tensor.transpose

            def banks_empty(p):
                for engine, s in (("a", emptied_a), ("d", emptied_d)):
                    if emptied(engine, p):
                        pe.wait_ge(s, emptied(engine, p))

            def turn(t):
                src, _ = TURNS[t]
                for b in range(4):
                    for k in (2 * b, 2 * b + 1):
                        for m in range(MT):
                            at = S * (k % 2) + P * m
                            last = turn_tile(banks[b][:, at:at + P], src[:, m, P * k:P * k + P], ident[:, :])
                    last.then_inc(turned, 1)

            def normed_turn(t, p):
                pe.wait_ge(xn_d, NORM_OF[t] + 1)
                pe.wait_ge(xn_a, NORM_OF[t] + 1)
                if p is not None:
                    banks_empty(p)
                turn(t)

            def hT_ready(t, k=KT - 1):
                pe.wait_ge(hT_d, 4 * t + k // 2 + 1)

            def product(psum, a, a_at, b, b_at, start, stop):
                for n, (i, j) in enumerate(((0, 0), (0, 1), (1, 0))):
                    last = mm(psum, a[i][a_at], b[j][b_at], start=(start and n == 0), stop=(stop and n == 2))
                return last

            h = (h_hi, h_lo)
            every = slice(None)

            def quarter(kind, j, c, fresh=None):
                p = AT[kind, j]
                w = parts(p)
                if c == 0:
                    if before_in_pair(p) is not None:
                        banks_empty(before_in_pair(p))
                b0 = pair_of(p)
                if kind in ("q", "k", "q2", "ff1", "xbc"):
                    for k in range(KT):
                        if c == 0 and k % 4 == 0:
                            pe.wait_ge(w_ready, 2 * p + k // 4 + 1)
                        if fresh is not None and c == 0 and k % 2 == 0:
                            hT_ready(fresh, max(k, 2 * b0 + 3))
                        last = product(banks[b0 + c // 2][:, S * (c % 2):S * (c % 2) + S], w, (every, k, slice(P * c, P * c + P)),
                                       h, (every, k, every), k == 0, k == KT - 1)
                else:
                    if c % 2 == 0:
                        pe.wait_ge(w_ready, 2 * p + c // 2 + 1)
                    if fresh is not None:
                        hT_ready(fresh, max(2 * c, 2 * b0 + 3))
                    for k in (2 * c, 2 * c + 1):
                        for m in range(MT):
                            last = product(banks[b0 + m][:, :], h, (every, k, slice(P * m, P * m + P)),
                                           w, (every, k, every), k == 0, k == KT - 1)
                if c == 3:
                    last.then_inc(panel_done, 1)

            def whole(kind, j, fresh=None):
                for c in range(4):
                    quarter(kind, j, c, fresh)

            def scores(n, q, k, k_tile):
                head = n % HEADS
                if n >= 2:
                    pe.wait_ge(scores_taken, n - 1)
                r = slice(DH * (head % 2), DH * (head % 2) + DH)
                bank = banks[4 + n % 2]
                mm(bank[:, 0:S], q[r, head // 2, P:S], k[r, k_tile, :], start=True, stop=True)
                mm(bank[:, S:S + P], q[r, head // 2, 0:P], k[r, k_tile, 0:P], start=True, stop=True).then_inc(scored, 1)

            def turn_probs(n):
                pe.wait_ge(probs_ready, n + 1)
                if n >= 2:
                    pe.wait_ge(heads_kept, n - 1)
                for c in range(3):
                    last = turn_tile(banks[6 + n % 2][:, P * c:P * c + P], soft[:, n % 2, P * c:P * c + P], ident[:, :])
                last.then_inc(probs_turned, 1)

            def values(n, v, c0):
                pe.wait_ge(softT_ready, n + 1)
                bank, b = banks[6 + n % 2], n % 2
                mm(bank[:, 384:448], softT[:, b, 256:384], v[:, 0, c0:c0 + DH], start=True, stop=True)
                mm(bank[:, 448:512], softT[:, b, 0:128], v[:, 0, c0:c0 + DH], start=True, stop=False)
                mm(bank[:, 448:512], softT[:, b, 128:256], v[:, 1, c0:c0 + DH], start=False, stop=True).then_inc(heads_out, 1)

            pe.wait_ge(consts_made, 1)
            pe.wait_ge(rows_loaded, 16 * len(ROWS))
            turn_tile(banks[4][:, 0:NROWS], small_rows, ident[0:NROWS, 0:NROWS]).then_inc(rows_turned, 1)
            normed_turn(T_MIX, None)
            whole("v", 0, T_MIX)
            pe.wait_ge(table_loaded, 16)
            pe.wait_ge(bucket_loaded, 16)
            pe.wait_ge(table_ones, 1)
            mm(banks[5][0:HEADS, 0:LINE], table[:, :], area(6)[0:BUCKETS + 1, 0:LINE], start=True, stop=True)\
                .then_inc(line_ready, 1)
            pe.wait_ge(ws_masked, 1)
            for g in range(GROUPS):
                last = turn_tile(banks[6 + g // 4][:, P * (g % 4):P * (g % 4) + P], w_s[:, g, :], ident[:, :])
            last.then_inc(ws_turned, 1)
            for kind, j in (("v", 1), ("u", 0), ("u", 1), ("q", 0), ("q", 1)):
                whole(kind, j)
            pe.wait_ge(wsT_ready, 1)
            pe.wait_ge(v_normed, 2)
            pe.wait_ge(cols_ready, 1)
            pe.wait_ge(line_copied, 1)
            for m in range(MT):
                for half in range(2):
                    for g in range(4 * half, 4 * half + 4):
                        last = mm(banks[4 + 2 * m + half][:, P * (g % 4):P * (g % 4) + P], w_sT[:, g, :],
                                  v_rows[:, m, P * g:P * g + P], start=True, stop=True)
                    last.then_inc(sgu_mixed, 1)
            for kind, j in (("k", 0), ("k", 1), ("va", 0), ("va", 1)):
                whole(kind, j)
            banks_empty(AT["va", 1])
            pe.wait_ge(ya_ready, 4)
            for step in range(HEADS + 2):
                if step < HEADS:
                    scores(step, qT, kT, step // 2)
                    quarter(("gb", "ga")[step // 8], (step // 4) % 2, step % 4)
                if 1 <= step <= HEADS:
                    turn_probs(step - 1)
                if step >= 2:
                    values(step - 2, va, DH * (step - 2))
            banks_empty(AT["ga", 1])
            pe.wait_ge(merged, 2)
            turn(T_MERGED)
            for j in range(2):
                whole("wo", j, T_MERGED if j == 0 else None)
            normed_turn(T_FFN, AT["wo", 1])
            for j in range(8):
                whole("ff1", j, T_FFN if j == 0 else None)
            banks_empty(AT["ff1", 7])
            pe.wait_ge(p_loaded, 16)
            for k in range(2):
                for m in range(MT):
                    last = turn_tile(banks[0][:, S * k + P * m:S * k + P * m + P], p_rows[:, m, P * k:P * k + P], ident[:, :])
            last.then_inc(p_turned, 1)
            for j in range(8):
                p = AT["ff2", j]
                pe.wait_ge(hid_ready, 4 * (j // 2) + 4)
                for k in range(KT):
                    if k % 4 == 0:
                        pe.wait_ge(w_ready, 2 * p + k // 4 + 1)
                    for m in range(MT):
                        last = product(banks[4 + 2 * m + j % 2][:, :], (hid_hi, hid_lo),
                                       (every, KT * (j // 2) + k, slice(P * m, P * m + P)), parts(p), (every, k, every),
                                       j < 2 and k == 0, j >= 6 and k == KT - 1)
                last.then_inc(panel_done, 1)
            pe.wait_ge(x_ready, X_MLP)
            p = AT["pp", 0]
            pe.wait_ge(w_ready, 2 * p + 2)
            pe.wait_ge(pT_ready, 1)
            for half in range(2):
                for m in range(MT):
                    for k in range(2):
                        last = product(banks[4 + 2 * m + half][:, :], (pT_hi, pT_lo), (every, k, slice(P * m, P * m + P)),
                                       parts(p), (every, k, slice(512 * half, 512 * half + 512)), k == 0, k == 1)
            last.then_inc(panel_done, 1)
            normed_turn(T_PLE, None)
            for j in range(2):
                whole("pg", j, T_PLE if j == 0 else None)
            normed_turn(T_MIX2, AT["pg", 1])
            hT_ready(T_MIX2)
            pe.wait_ge(x_ready, X_PLE)
            pe.wait_ge(dtw_ready, 1)
            for k in range(KT):
                last = product(banks[4][0:HEADS, 0:S], (dtw_hi, dtw_lo), (every, k, every), h, (every, k, every),
                               k == 0, k == KT - 1)
            last.then_inc(dt_made, 1)
            whole("q2", 0)
            pe.wait_ge(dt_kept, 1)
            for m in range(MT):
                last = turn_tile(banks[4][:, S + HEADS * m:S + HEADS * m + HEADS], dt_cols[:, P * m:P * m + P],
                                 ident[0:HEADS, 0:HEADS])
            last.then_inc(dt_turned, 1)
            whole("q2", 1)
            p = AT["kv2", 0]
            w, b0 = parts(p), pair_of(p)
            banks_empty(before_in_pair(p))
            pe.wait_ge(w_ready, 2 * p + 2)
            for g in range(2):
                for k in range(KT):
                    product(banks[b0][:, S * g:S * g + S], w, (every, k, slice(P * g, P * g + P)), h, (every, k, every),
                            k == 0, k == KT - 1)
            for m in range(MT):
                for k in range(KT):
                    last = product(banks[b0 + 1][:, P * m:P * m + P], h, (every, k, slice(P * m, P * m + P)),
                                   w, (every, k, slice(2 * P, 3 * P)), k == 0, k == KT - 1)
            last.then_inc(panel_done, 1)
            banks_empty(p)
            pe.wait_ge(dt_in, 1)
            for step in range(HEADS + 2):
                if step < HEADS:
                    scores(HEADS + step, q2T, k2T, step // 8)
                    quarter(*(("xbc", 0), ("xbc", 1), ("xbc", 2), ("z", 0))[step // 4], step % 4)
                else:
                    quarter("z", 1, step - HEADS)
                if 1 <= step <= HEADS:
                    turn_probs(HEADS + step - 1)
                if step >= 2:
                    values(HEADS + step - 2, v2, DH * ((step - 2) // 8))
            for c in (2, 3):
                quarter("z", 1, c)
            banks_empty(AT["z", 1])

            def project_out(j, first, last_one, quarters=range(4), fresh=None):
                p = AT["wo2", j]
                for k in (k for c in quarters for k in (2 * c, 2 * c + 1)):
                    if k % 4 == 0:
                        pe.wait_ge(w_ready, 2 * p + k // 4 + 1)
                    if fresh is not None and k % 2 == 0:
                        hT_ready(fresh, k)
                    for m in range(MT):
                        ins = product(banks[4 + 2 * m + j % 2][:, :], h, (every, k, slice(P * m, P * m + P)),
                                      parts(p), (every, k, every), first and k == 0, last_one and k == KT - 1)
                if quarters[-1] == 3:
                    ins.then_inc(panel_done, 1)

            pe.wait_ge(xc_ready, 3)
            for m in range(MT):
                for half in range(2):
                    for c in range(4):
                        last = turn_tile(banks[2 * m + half][:, P * c:P * c + P], xc[:, 4 * half + c, P * m:P * m + P],
                                         ident[:, :])
                    last.then_inc(x_turned, 1)
            pe.wait_ge(heads_kept, 2 * HEADS)
            pe.wait_ge(xtok_d, 2)
            pe.wait_ge(xtok_a, 2)
            pe.wait_ge(dt_ready, 1)
            a = dts[:, 5]
            for m in range(MT):
                mm(banks[0][:, HEADS * m:HEADS * m + HEADS], upper[:, :], a[:, m, :], start=True, stop=True)
            mm(banks[0][:, 32:48], ones[:, :], a[:, 0, :], start=True, stop=True)
            for g in range(SSD_G):
                last = turn_tile(banks[0][:, P + P * g:P + P * g + P], xc[:, 8 + g, 0:P], ident[:, :])
            last.then_inc(sums_made, 1)
            for m in range(MT):
                for g in range(SSD_G):
                    last = mm(banks[1][:, 256 * m + P * g:256 * m + P * g + P], xc[:, 8 + g, P * m:P * m + P],
                              xc[:, 10 + g, P * m:P * m + P], start=True, stop=True)
            last.then_inc(cb_made, 1)
            pe.wait_ge(sums_ready, 1)
            pe.wait_ge(cb_ready, 1)
            pe.wait_ge(att_ready, 1)
            turn(T_ATT)
            hT_ready(T_ATT)

            def diagonal(m):
                pe.wait_ge(xdt_ready, 1)
                if m:
                    pe.wait_ge(diag_taken, m)
                for n in range(HEADS):
                    if n % 4 == 0:
                        pe.wait_ge(decay_ready, 4 * m + n // 4 + 1)
                    last = mm(banks[2 + n // 8][:, DH * (n % 8):DH * (n % 8) + DH], decay[:, n, :],
                              xdt[:, m, DH * n:DH * n + DH], start=True, stop=True)
                last.then_inc(diag_made, 1)

            for m in range(MT):
                for q in range(4):
                    n = 4 * m + q
                    if n >= 2:
                        pe.wait_ge(seg_ready, n - 1)
                    for i in range(4):
                        last = mm(banks[n % 2][:, P * i:P * i + P], a[:, m, 4 * q + i:4 * q + i + 1].to_broadcast([P, P]),
                                  upper[:, :], start=True, stop=True)
                    last.then_inc(seg_made, 1)
                    if q % 2:
                        project_out(2, True, False, range(2 * m + q // 2, 2 * m + q // 2 + 1))
                diagonal(m)
            pe.wait_ge(xde_ready, 1)
            pe.wait_ge(seg_ready, 8)
            for g in range(SSD_G):
                last = mm(banks[g][:, :], b_tok[:, g, :], xde[:, 512 * g:512 * g + 512], start=True, stop=True)
            last.then_inc(state_made, 1)
            pe.wait_ge(state_ready, 1)
            pe.wait_ge(diag_taken, 2)
            for g in range(SSD_G):
                last = mm(banks[2 + g][:, :], xc[:, 10 + g, P:S], state[:, 512 * g:512 * g + 512], start=True, stop=True)
            last.then_inc(off_made, 1)
            project_out(3, True, False)
            pe.wait_ge(y_gated, 2)
            turn(T_SSD)
            for j in range(2):
                project_out(j, False, True, fresh=T_SSD if j == 0 else None)
            normed_turn(T_FFN2, None)
            pe.wait_ge(hT_d, 4 * T_FFN2 + 2)
            pe.wait_ge(hT_a, 4 * T_FFN2 + 2)
            pe.wait_ge(router_loaded, 32)
            for m in range(MT):
                for k in range(KT):
                    last = mm(banks[0][:, 72 * m:72 * m + 72], hT[:, k, P * m:P * m + P], routerw[:, k, :],
                              start=(k == 0), stop=(k == KT - 1))
            last.then_inc(routed, 1)
            pe.wait_ge(zeros_made, 1)
            for b in range(4):
                mm(banks[4 + b][:, :], zeros[:, 0:P], zeros, start=True, stop=False)
            pe.wait_ge(marks_ready, 1)
            marks = one_hot[:, 2]
            mm(banks[1][:, 0:NE], above[:, :], marks[:, 0, :], start=True, stop=True)
            mm(banks[1][:, NE:2 * NE], ones[:, :], marks[:, 0, :], start=True, stop=False)
            mm(banks[1][:, NE:2 * NE], above[:, :], marks[:, 1, :], start=False, stop=True)
            mm(banks[1][:, 2 * NE:3 * NE], ones[:, :], marks[:, 0, :], start=True, stop=False)
            mm(banks[1][:, 2 * NE:3 * NE], ones[:, :], marks[:, 1, :], start=False, stop=True).then_inc(ranks_made, 1)
            pe.wait_ge(marks_done, 1)
            fullest = pe.value_load(count_i[0:1, NE:NE + 1], min_val=0, max_val=S)

            def gather(i):
                pe.wait_ge(picked, i + 1)
                for b in range(2):
                    for k in range(4):
                        for m in range(MT):
                            last = mm(banks[b][:, P * k:P * k + P], t_rows[:, m, P * (4 * b + k):P * (4 * b + k) + P],
                                      pick[:, m, :, :].rearrange("p e s -> p (e s)"), start=(m == 0), stop=(m == MT - 1))
                    last.then_inc(gathered, 1)

            def experts(half_i, odd, last_one=False):
                i = 2 * half_i + odd
                pe.wait_ge(xe_a, i + 1)
                pe.wait_ge(xe_d, i + 1)
                for w, bank, done in (("gate", banks[2], gated), ("up", banks[3], upped)):
                    for e in range(2):
                        if w == "gate":
                            pe.wait_ge(pair_landed["odd_gate" if odd else w, e], 16 * (half_i + 1))
                        else:
                            pe.wait_ge(pair_landed[w, e], 16 * (i + 1))
                    for k in range(KT):
                        for e in range(2):
                            last = mm(bank[SLOTS * e:SLOTS * e + SLOTS, :], xeT[:, k, SLOTS * e:SLOTS * e + SLOTS],
                                      expert_panel(w, e, odd)[:, k, :], start=(k == 0), stop=(k == KT - 1))
                    last.then_inc(done, 1)
                pe.wait_ge(picked_g, i + 1)
                for m in range(MT):
                    last = turn_tile(banks[1][:, P * m:P * m + P], pick_g[:, m, :, :].rearrange("p e s -> p (e s)"),
                                     ident[:, :])
                last.then_inc(put_turned, 1)
                pe.wait_ge(he_ready, i + 1)
                for c in range(4):
                    last = turn_tile(banks[0][:, P * c:P * c + P], h_e[:, P * c:P * c + P], ident[:, :])
                last.then_inc(he_turned, 1)
                pe.wait_ge(heT_ready, i + 1)
                pe.wait_ge(put_ready, i + 1)
                if not last_one:
                    gather(i + 1)
                for e in range(2):
                    pe.wait_ge(pair_landed["down", e], 16 * (i + 1))
                for c in range(4):
                    for half in range(2):
                        for e in range(2):
                            last = mm(banks[2 + half][SLOTS * e:SLOTS * e + SLOTS, :], heT[:, c, SLOTS * e:SLOTS * e + SLOTS],
                                      expert_panel("down", e, odd)[:, c, 512 * half:512 * half + 512],
                                      start=(c == 0), stop=(c == 3))
                last.then_inc(downed, 1)
                pe.wait_ge(ye_a, i + 1)
                pe.wait_ge(ye_d, i + 1)
                for m in range(MT):
                    for half in range(2):
                        last = mm(banks[4 + 2 * m + half][:, :], put[:, m, :], y_e[:, 512 * half:512 * half + 512],
                                  start=False, stop=False)
                last.then_inc(scattered, 1)

            def two_rounds(half_i, last_two=False):
                experts(half_i, 0)
                experts(half_i, 1, last_two)

            gather(0)
            with pe.Fori(0, PAIRS // 2 - 1) as i:
                two_rounds(i)
            two_rounds(PAIRS // 2 - 1, True)
            with pe.If(fullest > SLOTS):
                with pe.Fori(1, PASSES) as r:
                    gather(r * PAIRS)
                    with pe.Fori(0, PAIRS // 2 - 1) as j:
                        two_rounds(r * (PAIRS // 2) + j)
                    two_rounds(r * (PAIRS // 2) + (PAIRS // 2 - 1), True)
            for b in range(4):
                last = mm(banks[4 + b][:, :], zeros[:, 0:P], zeros, start=False, stop=True)
            last.then_inc(y_summed, 1)

        @block.vector
        def _(dve):
            link = linker(dve, dve_step)
            tt, ts, stt = nc.vector.tensor_tensor, nc.vector.tensor_scalar, nc.vector.scalar_tensor_tensor
            copy, recip = nc.vector.tensor_copy, nc.vector.reciprocal
            norms = [0]

            def sum_squares(src, n, squared, first=1):
                for i in range(D // n):
                    part = slice(n * i, n * i + n)
                    last = nc.vector.tensor_tensor_reduce(squared[:, 1, part], src[:, 1, part], src[:, 1, part], 1.0, 0.0,
                                                          ALU.mult, ALU.add, stats[:, first + i:first + i + 1])
                link(last)

            def rstd(n_stats, width):
                norms[0] += 1
                dve.wait_ge(squares, norms[0])
                ts(stats[:, 4:4 + n_stats], stats[:, 0:n_stats], 1.0 / width, EPS, ALU.mult, ALU.add).then_inc(mean_ready, 1)
                dve.wait_ge(root_ready, norms[0])
                recip(stats[:, 8:8 + n_stats], stats[:, 4:4 + n_stats]).then_inc(rstd_ready, 1)
                dve.wait_ge(rstd_ready, norms[0])

            def norm_x(t):
                if t == T_MIX:
                    dve.wait_ge(x_loaded, 16)
                elif t == T_FFN:
                    dve.wait_ge(emptied_d, emptied("d", AT["wo", 1]))
                else:
                    dve.wait_ge(x_ready, {T_PLE: X_MLP, T_FFN2: X_MIX2}[t])
                sum_squares(x, D, xn)
                rstd(MT, D)
                ts(xn[:, 0, :], x[:, 0, :], stats[:, 8:9], None, ALU.mult).then_inc(xn_d, 1)

            def turn(t):
                _, gain = TURNS[t]
                for b in (0, 2) if t == T_FFN2 else range(4):
                    if t == T_FFN2:
                        dve.wait_ge(turned, 4 * t + b + 1)
                    else:
                        dve.wait_ge(hT_a, 4 * t + b + 1)
                    for k in (2 * b, 2 * b + 1):
                        psum = banks[b][:, S * (k % 2):S * (k % 2) + S]
                        if t == T_FFN2:
                            last = ts(hT[:, k, :], psum, col(gain, k), None, ALU.mult)
                        elif gain:
                            last = stt(h_lo[:, k, :], psum, col(gain, k), h_hi[:, k, :], ALU.mult, ALU.subtract)
                        else:
                            last = tt(h_lo[:, k, :], psum, h_hi[:, k, :], ALU.subtract)
                    last.then_inc(hT_d, 1)

            def split(*halves):
                for q in halves:
                    dve.wait_ge(w_rounded, q + 1)
                    for source, hi, lo in pieces(q):
                        last = tt(lo, source, hi, ALU.subtract)
                    last.then_inc(w_ready, 1)

            def split_panel(p):
                split(2 * p, 2 * p + 1)

            def hidden(j, next_split):
                dve.wait_ge(emptied_a, emptied("a", AT["ff1", j]))
                for b in range(2):
                    part = hid[:, 1024 * (j % 2) + 512 * b:1024 * (j % 2) + 512 * b + 512]
                    tt(part, part, part, ALU.mult).then_inc(hid_squared, 1)
                split_panel(next_split)
                for b in range(2):
                    part = hid[:, 1024 * (j % 2) + 512 * b:1024 * (j % 2) + 512 * b + 512]
                    rounded, rest = (v[:, 4 * j + 2 * b:4 * j + 2 * b + 2, :].rearrange("p k t -> p (k t)") for v in (hid_hi, hid_lo))
                    dve.wait_ge(hid_squared, 2 * j + b + 1)
                    dve.wait_ge(hid_rounded, 2 * j + b + 1)
                    tt(rest, part, rounded, ALU.subtract).then_inc(hid_ready, 1)

            def empty(kind, j):
                p = AT[kind, j]
                dve.wait_ge(panel_done, p + 1)
                for b, engine in enumerate(EMPTIED_BY[kind]):
                    if engine != "d":
                        continue
                    bank = banks[pair_of(p) + b]
                    half = slice(512 * j, 512 * j + 512)
                    if kind in ("q", "k", "q2"):
                        dst = {"q": qT, "k": kT, "q2": q2T}[kind][:, 4 * j + 2 * b:4 * j + 2 * b + 2, :]
                        ins = ts(dst.rearrange("p k t -> p (k t)"), bank[:, :], 1.0 if kind == "k" else Q_SCALE, None, ALU.mult)
                    elif kind == "va":
                        ins = copy(va[:, b, half], bank[:, :])
                    elif kind == "wo":
                        ins = tt(x[:, b, half], bank[:, :], x[:, b, half], ALU.add)
                    elif kind == "kv2":
                        ins = copy(v2.rearrange("p m c -> p (m c)"), bank[:, 0:S])
                    elif kind == "xbc":
                        ins = copy(xraw[:, 4 * j + 2 * b:4 * j + 2 * b + 2, TAPS - 1:],
                                   bank[:, :].rearrange("p (c t) -> p c t", c=2))
                    ins.then_inc(emptied_d, 1)

            def head_scores(n):
                b, h, bank = n % 2, n % HEADS, banks[4 + n % 2]
                dve.wait_ge(scored, n + 1)
                if n >= 2:
                    dve.wait_ge(probs_turned, n - 1)
                mask = bias[:, h, ::-1] if n < HEADS else window[:, :]
                own = bias[:, h, P - 1::-1] if n < HEADS else window[:, P:S]
                tt(soft[:, b, 0:S], bank[:, 0:S], mask, ALU.add)
                tt(soft[:, b, S:384], bank[:, S:384], own, ALU.add).then_inc(scores_taken, 1)
                dve.wait_ge(scores_taken, n + 1)
                nc.vector.tensor_reduce(peak[:, n % 4, 0:1], soft[:, b, 0:S], AX_X, ALU.max, negate=True)
                last = nc.vector.tensor_reduce(peak[:, n % 4, 1:2], soft[:, b, S:384], AX_X, ALU.max, negate=True)
                if n >= HEADS:
                    link(last)
                    last = ts(peak[:, n % 4, 0:2], peak[:, n % 4, 0:2], neg_sink[:, h:h + 1], None, ALU.min)
                last.then_inc(peak_ready, 1)

            def head_output(n, dst):
                b, h = n % 2, n % HEADS
                dve.wait_ge(probs_ready, n + 1)
                if n >= HEADS:
                    link(tt(head_sum[:, n % 4, 0:2], head_sum[:, n % 4, 0:2], sink_e[:, n % 4, :], ALU.add))
                link(recip(head_sum[:, n % 4, 2:4], head_sum[:, n % 4, 0:2]))
                dve.wait_ge(heads_out, n + 1)
                bank = banks[6 + b]
                ts(dst[:, 0, DH * h:DH * h + DH], bank[:, 384:448], head_sum[:, n % 4, 3:4], None, ALU.mult)
                ts(dst[:, 1, DH * h:DH * h + DH], bank[:, 448:512], head_sum[:, n % 4, 2:3], None, ALU.mult).then_inc(heads_kept, 1)

            nc.vector.memset(table[BUCKETS:BUCKETS + 1, :], 1.0).then_inc(table_ones, 1)
            norm_x(T_MIX)
            dve.wait_ge(rows_turned, 1)
            copy(cols[:, :], banks[4][:, 0:NROWS]).then_inc(cols_ready, 1)
            dve.wait_ge(cols_ready, 1)
            split(0)
            turn(T_MIX)
            split(1)
            split_panel(1)
            dve.wait_ge(line_ready, 1)
            copy(soft[0:HEADS, :, :].rearrange("p a b -> p (a b)")[:, 0:LINE], banks[5][0:HEADS, :]).then_inc(line_copied, 1)
            dve.wait_ge(ws_turned, 1)
            copy(w_sT[:, 0:4, :].rearrange("p g t -> p (g t)"), banks[6][:, :])
            copy(w_sT[:, 4:8, :].rearrange("p g t -> p (g t)"), banks[7][:, :]).then_inc(wsT_ready, 1)
            split_panel(AT["u", 0])
            dve.wait_ge(emptied_a, emptied("a", AT["v", 1]))
            for m in range(MT):
                vm, mean, var = v_rows[:, m, :], stats[:, 12 + m:13 + m], stats[:, 14 + m:15 + m]
                link(nc.vector.tensor_reduce(mean, vm, AX_X, ALU.add))
                link(ts(mean, mean, -1.0 / D, None, ALU.mult))
                link(ts(vm, vm, mean, None, ALU.add))
                link(tt(xn[:, m, :], vm, vm, ALU.mult))
                link(nc.vector.tensor_reduce(var, xn[:, m, :], AX_X, ALU.add))
            ts(stats[:, 14:16], stats[:, 14:16], 1.0 / D, EPS, ALU.mult, ALU.add).then_inc(v_mean, 1)
            split_panel(AT["u", 1])
            split_panel(AT["q", 0])
            dve.wait_ge(ln_loaded, 32)
            dve.wait_ge(v_root, 1)
            link(recip(stats[:, 14:16], stats[:, 14:16]))
            for m in range(MT):
                vm = v_rows[:, m, :]
                link(stt(vm, vm, stats[:, 14 + m:15 + m], ln_vecs[:, 0, :], ALU.mult, ALU.mult))
                tt(vm, vm, ln_vecs[:, 1, :], ALU.add).then_inc(v_normed, 1)
            split_panel(AT["q", 1])
            for j in range(2):
                empty("q", j)
                split_panel(AT["q", j] + 2)
            dve.wait_ge(emptied_a, emptied("a", AT["u", 1]))
            for m in range(MT):
                for half in range(2):
                    dve.wait_ge(sgu_mixed, 2 * m + half + 1)
                    for g in range(4 * half, 4 * half + 4):
                        u = u_rows[:, m, P * g:P * g + P]
                        last = stt(u, banks[4 + 2 * m + half][:, P * (g % 4):P * (g % 4) + P], col("b_sgu", g), u,
                                   ALU.add, ALU.mult)
                    last.then_inc(ya_ready, 1)
            for kind in ("k", "va"):
                for j in range(2):
                    empty(kind, j)
                    if (kind, j) != ("va", 1):
                        split_panel(AT[kind, j] + 2)
            dve.wait_ge(bias_loaded, 16)

            def merge(half):
                at = slice(512 * half, 512 * half + 512)
                dve.wait_ge(emptied_a, emptied("a", AT["ga", half]))
                dve.wait_ge(heads_kept, 8 * half + 8)
                dve.wait_ge(ya_ready, 4)
                tt(u_rows[:, :, at], u_rows[:, :, at], sga[:, :, at], ALU.mult)
                link(tt(yb[:, :, at], yb[:, :, at], sgb[:, :, at], ALU.mult))
                tt(yb[:, :, at], yb[:, :, at], u_rows[:, :, at], ALU.add).then_inc(merged, 1)

            for step in range(HEADS + 2):
                if step < HEADS:
                    head_scores(step)
                if step >= 2:
                    head_output(step - 2, yb)
                if step - 1 in SPLIT_AT:
                    split(2 * AT["gb", 1] + SPLIT_AT.index(step - 1))
                if step == 13:
                    merge(0)
            merge(1)
            turn(T_MERGED)
            split_panel(AT["wo", 1])
            empty("wo", 0)
            split_panel(AT["ff1", 0])
            empty("wo", 1)
            norm_x(T_FFN)
            turn(T_FFN)
            split_panel(AT["ff1", 1])
            for j in range(8):
                hidden(j, AT["ff1", j] + 2)
            dve.wait_ge(pT_rounded, 1)
            tt(pT_lo.rearrange("p k t -> p (k t)"), banks[0][:, :], pT_hi.rearrange("p k t -> p (k t)"), ALU.subtract)\
                .then_inc(pT_ready, 1)
            for p in range(AT["ff2", 2], AT["pg", 0]):
                split_panel(p)
            dve.wait_ge(panel_done, AT["ff2", 7] + 1)
            for b in range(4):
                part = x[:, b // 2, 512 * (b % 2):512 * (b % 2) + 512]
                tt(part, banks[4 + b][:, :], part, ALU.add).then_inc(x_ready, 1)
            norm_x(T_PLE)
            split(2 * AT["pg", 0])
            turn(T_PLE)
            split(2 * AT["pg", 0] + 1)
            split_panel(AT["pg", 1])
            dve.wait_ge(dtw_rounded, 1)
            tt(dtw_lo[:, :, :], dtw[:, :, :], dtw_hi[:, :, :], ALU.subtract).then_inc(dtw_ready, 1)
            split_panel(AT["q2", 0])
            for half in range(2):
                at = slice(512 * half, 512 * half + 512)
                dve.wait_ge(emptied_a, emptied("a", AT["pg", half]))
                for m in range(MT):
                    last = tt(gate_rows[:, m, at], banks[4 + 2 * m + half][:, :], gate_rows[:, m, at], ALU.mult)
                link(last)
                tt(x[:, :, at], x[:, :, at], gate_rows[:, :, at], ALU.add).then_inc(x_ready, 2)
                dve.wait_ge(x_ready, X_MLP + 2 * half + 2)
                dve.wait_ge(final_loaded, 16)
                tt(xg[:, :, at], x[:, :, at], final_g[:, at].unsqueeze(1).to_broadcast([P, MT, 512]), ALU.mult)\
                    .then_inc(xg_ready, 1)
            sum_squares(x, D, rows_area(3))
            dve.wait_ge(xg_ready, 2)
            sum_squares(xg, D, rows_area(2), 3)
            r1, r2 = stats[:, 8:10], stats[:, 10:12]
            norms[0] += 2
            dve.wait_ge(squares, norms[0])
            link(ts(stats[:, 4:6], stats[:, 0:2], 1.0 / D, EPS, ALU.mult, ALU.add))
            link(recip(stats[:, 12:14], stats[:, 4:6]))
            link(tt(stats[:, 6:8], stats[:, 2:4], stats[:, 12:14], ALU.mult))
            ts(stats[:, 6:8], stats[:, 6:8], 1.0 / D, EPS, ALU.mult, ALU.add).then_inc(mean_ready, 2)
            dve.wait_ge(root_ready, norms[0])
            link(recip(stats[:, 8:12], stats[:, 4:8]))
            tt(r2, r2, r1, ALU.mult).then_inc(rstd_ready, 2)
            dve.wait_ge(rstd_ready, norms[0])
            ts(xn[:, 0, :], xg[:, 0, :], r2[:, 0:1], None, ALU.mult).then_inc(xn_d, 1)
            turn(T_MIX2)
            dve.wait_ge(dt_made, 1)
            copy(dt_cols, banks[4][0:HEADS, 0:S]).then_inc(dt_kept, 1)
            split_panel(AT["q2", 1])
            for j in range(2):
                empty("q2", j)
                split_panel(AT["q2", j] + 2)
            empty("kv2", 0)
            dve.wait_ge(heads_loaded, 64)
            dve.wait_ge(dt_turned, 1)
            link(tt(dts[:, 0], banks[4][:, S:S + 32].rearrange("p (m h) -> p m h", m=MT),
                    heads4[:, 0:1, :].to_broadcast([P, MT, HEADS]), ALU.add))
            stt(dts[:, 1], dts[:, 0], -1.0, dts[:, 0], ALU.mult, ALU.max).then_inc(dt_in, 1)
            ts(neg_sink[:, :], heads4[:, 3, :], -1.0, None, ALU.mult).then_inc(sink_ready, 1)
            dve.wait_ge(sink_ready, 1)
            dve.wait_ge(dt_exp, 1)
            ts(dts[:, 3], dts[:, 2], 1.0, None, ALU.add).then_inc(dt_in, 1)
            dve.wait_ge(dt_in, 2)
            link(ts(dts[:, 10], dts[:, 3], 1.0, None, ALU.subtract))
            link(ts(dts[:, 11], dts[:, 10], 0.0, None, ALU.is_equal))
            dve.wait_ge(dt_log, 1)
            tt(dts[:, 12], dts[:, 4], dts[:, 11], ALU.add)
            link(tt(dts[:, 10], dts[:, 10], dts[:, 11], ALU.add))
            link(recip(dts[:, 13], dts[:, 10]))
            link(tt(dts[:, 12], dts[:, 12], dts[:, 13], ALU.mult))
            link(tt(dts[:, 12], dts[:, 12], dts[:, 2], ALU.mult))
            link(ts(dts[:, 13], dts[:, 0], 0.0, None, ALU.max))
            link(tt(dts[:, 0], dts[:, 12], dts[:, 13], ALU.add))
            dve.wait_ge(w_exp, 1)
            stt(dts[:, 5], dts[:, 0], -1.0, heads4[:, 1:2, :].to_broadcast([P, MT, HEADS]), ALU.mult, ALU.mult)\
                .then_inc(dt_ready, 1)

            def conv(c):
                j = c // 4
                dve.wait_ge(emptied_a, emptied("a", AT["xbc", j]))
                dve.wait_ge(emptied_d, emptied("d", AT["xbc", j]))
                if c == 0:
                    dve.wait_ge(pads_zero, 1)
                last = ts(xc[:, c, :], xraw[:, c, 3:3 + S], col("conv_w", 3 * CT + c), col("conv_b", c), ALU.mult, ALU.add)
                for tap in range(TAPS - 1):
                    link(last)
                    last = stt(xc[:, c, :], xraw[:, c, tap:tap + S], col("conv_w", tap * CT + c), xc[:, c, :],
                               ALU.mult, ALU.add)
                last.then_inc(conv_ready, 1)

            for step in range(HEADS + 2):
                if step < HEADS:
                    head_scores(HEADS + step)
                if step >= 2:
                    head_output(HEADS + step - 2, att)
                if step % 4 == 3 and step < 12:
                    empty("xbc", step // 4)
                if step - 1 in SPLIT_AT:
                    split(2 * AT["xbc", 1] + SPLIT_AT.index(step - 1))
                if 5 <= step < 5 + CT:
                    conv(step - 5)
            split_panel(AT["wo2", 2])
            dve.wait_ge(heads_kept, 2 * HEADS)
            sum_squares(att, D, rows_area(0))
            rstd(MT, D)
            for m in range(MT):
                last = ts(att[:, m, :], att[:, m, :], stats[:, 8 + m:9 + m], None, ALU.mult)
            last.then_inc(att_ready, 1)
            for b in (0, 2):
                dve.wait_ge(x_turned, b + 1)
                copy(xtok[:, b // 2, 0:512], banks[b][:, :]).then_inc(xtok_d, 1)
            dve.wait_ge(xtok_a, 2)
            dve.wait_ge(xtok_d, 2)
            by_head = lambda rows: rows.rearrange("p (h d) -> p h d", h=HEADS)
            spread = lambda v: v.unsqueeze(2).to_broadcast([P, HEADS, DH])
            for m in range(MT):
                last = tt(by_head(xdt[:, m, :]), by_head(xtok[:, m, :]), spread(dts[:, 0, m, :]), ALU.mult)
            last.then_inc(xdt_ready, 1)
            for m in range(MT):
                link(tt(by_head(y[:, m, :]), by_head(xtok[:, m, :]), spread(heads4[:, 2, :]), ALU.mult))
            dve.wait_ge(sums_made, 1)
            copy(dts[:, 14, 0], banks[0][:, 32:48])
            copy(b_tok.rearrange("p g n -> p (g n)"), banks[0][:, P:P + 256])
            link(copy(dts[:, 6].rearrange("p m h -> p (m h)"), banks[0][:, 0:32]))
            tt(dts[:, 7, 0], dts[:, 14, 0], dts[:, 6, 0], ALU.subtract).then_inc(sums_ready, 1)
            dve.wait_ge(cb_made, 1)
            tt(cbm.rearrange("p m g l -> p (m g) l"), banks[1][:, :].rearrange("p (n l) -> p n l", n=4),
               upper[:, :].unsqueeze(1).to_broadcast([P, 4, P]), ALU.mult).then_inc(cb_ready, 1)
            turn(T_ATT)
            dve.wait_ge(end_exp, 1)
            dve.wait_ge(xdt_ready, 1)
            tt(by_head(xde), by_head(xdt[:, 0, :]), spread(dts[:, 9, 0]), ALU.mult).then_inc(xde_ready, 1)
            dve.wait_ge(cb_ready, 1)

            def segments(n):
                m, q = n // 4, n % 4
                dve.wait_ge(seg_made, n + 1)
                if m:
                    dve.wait_ge(diag_made, m)
                for h in range(4):
                    last = ts(decay[:, 4 * q + h, :], banks[n % 2][:, P * h:P * h + P], dts[:, 6, m, 4 * q + h:4 * q + h + 1],
                              0.0, ALU.subtract, ALU.min)
                last.then_inc(seg_ready, 1)

            def decays(n):
                m, q = n // 4, n % 4
                dve.wait_ge(decay_exp, n + 1)
                part = decay[:, 4 * q:4 * q + 4, :]
                tt(part, part, cbm[:, m, q // 2:q // 2 + 1, :].to_broadcast([P, 4, P]), ALU.mult).then_inc(decay_ready, 1)

            for m in range(MT):
                for q in range(4):
                    segments(4 * m + q)
                    if q:
                        decays(4 * m + q - 1)
                decays(4 * m + 3)
                if m == 0:
                    split_panel(AT["wo2", 3])
                dve.wait_ge(diag_made, m + 1)
                for half in range(2):
                    part = y[:, m, 512 * half:512 * half + 512]
                    last = tt(part, banks[2 + half][:, :], part, ALU.add)
                last.then_inc(diag_taken, 1)
            dve.wait_ge(off_made, 1)
            dve.wait_ge(diag_taken, 2)
            for half in range(2):
                hs = slice(8 * half, 8 * half + 8)
                link(tt(xde[:, 512 * half:512 * half + 512].rearrange("p (h d) -> p h d", h=8),
                            banks[2 + half][:, :].rearrange("p (h d) -> p h d", h=8),
                            dts[:, 8, 1, hs].unsqueeze(2).to_broadcast([P, 8, DH]), ALU.mult))
            link(tt(y[:, 1, :], y[:, 1, :], xde, ALU.add))
            dve.wait_ge(emptied_a, emptied("a", AT["z", 1]))
            for m in range(MT):
                last = tt(y[:, m, :], y[:, m, :], sz[:, m, :], ALU.mult)
            last.then_inc(y_gated, 1)
            split_panel(AT["wo2", 0])
            dve.wait_ge(y_gated, 1)
            sum_squares(y, D // SSD_G, xtok, 2)
            rstd(4, D // SSD_G)
            for m in range(MT):
                for g in range(SSD_G):
                    part = y[:, m, 512 * g:512 * g + 512]
                    last = ts(part, part, stats[:, 8 + 2 * m + g:9 + 2 * m + g], None, ALU.mult)
            last.then_inc(y_gated, 1)
            turn(T_SSD)
            split_panel(AT["wo2", 1])
            dve.wait_ge(panel_done, NP)
            dve.wait_ge(x_ready, X_OUT1)
            for b in range(4):
                part = x[:, b // 2, 512 * (b % 2):512 * (b % 2) + 512]
                tt(part, banks[4 + b][:, :], part, ALU.add).then_inc(x_ready, 1)
            norm_x(T_FFN2)
            turn(T_FFN2)
            dve.wait_ge(xn_d, 5)
            dve.wait_ge(xn_a, 5)
            dve.wait_ge(gains_loaded, 32)
            for m in range(MT):
                last = tt(t_rows[:, m, :], xn[:, m, :], gains[:, 0, :], ALU.mult)
            last.then_inc(t_ready, 1)
            dve.wait_ge(consts_made, 1)
            dve.wait_ge(routed, 1)
            link(copy(logits.rearrange("p m e -> p (m e)"), banks[0][:, 0:144]))
            eight = [P, MT, EG]

            by_group = one_hot[:, 5].rearrange("p m (g e) -> p m g e", g=EG)

            def first_of(values, at):
                top = rt[:, at + 1, :, 0:1]
                link(nc.vector.tensor_reduce(rt[:, at + 1, :, 0], values, AX_X, ALU.max))
                link(tt(rt[:, at + 2], values, top.to_broadcast(eight), ALU.is_lt))
                link(stt(rt[:, at + 2], rt[:, at + 2], 1000.0, iota[:, 0:EG].unsqueeze(1).to_broadcast(eight),
                         ALU.mult, ALU.add))
                link(nc.vector.tensor_reduce(rt[:, at + 3, :, 0], rt[:, at + 2], AX_X, ALU.min))
                link(tt(rt[:, at], iota[:, 0:EG].unsqueeze(1).to_broadcast(eight), rt[:, at + 3, :, 0:1].to_broadcast(eight),
                        ALU.is_equal))

            groups = logits[:, :, 0:EG]
            first_of(groups, 20)
            link(tt(rt[:, 2], groups, rt[:, 21, :, 0:1].to_broadcast(eight), ALU.subtract))
            link(tt(by_group, logits[:, :, EG:].rearrange("p m (g e) -> p m g e", g=EG),
                    rt[:, 20].unsqueeze(3).to_broadcast([P, MT, EG, EG]), ALU.mult))
            link(nc.vector.tensor_reduce(rt[:, 4], by_group.rearrange("p m g e -> p m e g"), AX_X, ALU.add))
            first_of(rt[:, 4], 24)
            link(stt(rt[:, 6], rt[:, 24], -3e38, rt[:, 4], ALU.mult, ALU.add))
            first_of(rt[:, 6], 28)
            tt(rt[:, 12, :, 0:1], rt[:, 29, :, 0:1], rt[:, 25, :, 0:1], ALU.subtract).then_inc(route_max, 1)
            dve.wait_ge(route_exp, 1)
            link(nc.vector.tensor_reduce(rt[:, 7, :, 0], rt[:, 3], AX_X, ALU.add))
            link(recip(rt[:, 8, :, 0:1], rt[:, 7, :, 0:1]))
            link(ts(rt[:, 9, :, 0:1], rt[:, 13, :, 0:1], 1.0, None, ALU.add))
            link(recip(rt[:, 10, :, 0:1], rt[:, 9, :, 0:1]))
            link(tt(rt[:, 10, :, 0:1], rt[:, 10, :, 0:1], rt[:, 8, :, 0:1], ALU.mult))
            link(tt(rt[:, 11, :, 0:1], rt[:, 10, :, 0:1], rt[:, 13, :, 0:1], ALU.mult))
            link(tt(rt[:, 14], rt[:, 24], rt[:, 28], ALU.add))
            link(tt(rt[:, 15], rt[:, 24], rt[:, 10, :, 0:1].to_broadcast(eight), ALU.mult))
            link(tt(rt[:, 16], rt[:, 28], rt[:, 11, :, 0:1].to_broadcast(eight), ALU.mult))
            link(tt(rt[:, 15], rt[:, 15], rt[:, 16], ALU.add))
            for n, values in ((2, rt[:, 14]), (3, rt[:, 15])):
                last = tt(one_hot[:, n].rearrange("p m (g e) -> p m g e", g=EG),
                          rt[:, 20].unsqueeze(3).to_broadcast([P, MT, EG, EG]),
                          values.unsqueeze(2).to_broadcast([P, MT, EG, EG]), ALU.mult)
            last.then_inc(marks_ready, 1)
            dve.wait_ge(ranks_made, 1)
            dve.wait_ge(marks_ready, 1)
            place = one_hot[:, 4]
            link(stt(place, banks[1][:, 0:2 * NE].rearrange("p (m e) -> p m e", m=MT), 1.0, one_hot[:, 2], ALU.add, ALU.mult))
            link(ts(place, place, -1.0, None, ALU.add))
            link(nc.vector.tensor_reduce(rt[:, 17, 0, 0:1], banks[1][:, 2 * NE:3 * NE], AX_X, ALU.max))
            copy(count_i[:, 0:NE], banks[1][:, 2 * NE:3 * NE])
            copy(count_i[:, NE:NE + 1], rt[:, 17, 0, 0:1]).then_inc(marks_done, 1)
            dve.wait_ge(marks_done, 1)
            dve.wait_ge(t_ready, 1)
            fullest = dve.value_load(count_i[0:1, NE:NE + 1], min_val=0, max_val=S)
            slots4 = iota[:, :].unsqueeze(1).unsqueeze(1).to_broadcast([P, MT, 2, SLOTS])

            def choose(i, pair, first=False):
                if not first:
                    dve.wait_ge(gathered, 2 * i)
                    dve.wait_ge(picked_g, i)
                at = bass.ds(pair * 2, 2)
                tt(pick, slots4, place[:, :, at].unsqueeze(3).to_broadcast([P, MT, 2, SLOTS]), ALU.is_equal).then_inc(picked, 1)

            def choose_gates(i, pair):
                at = bass.ds(pair * 2, 2)
                dve.wait_ge(picked, i + 1)
                tt(pick_g, pick, one_hot[:, 3][:, :, at].unsqueeze(3).to_broadcast([P, MT, 2, SLOTS]), ALU.mult).then_inc(picked_g, 1)

            def gather(i):
                dve.wait_ge(gathered, 2 * i + 2)
                copy(xeT[:, 4:8, :].rearrange("p k s -> p (k s)"), banks[1][:, :]).then_inc(xe_d, 1)

            def experts(i, pair, last=False):
                if not last:
                    choose(i + 1, pair + 1)
                dve.wait_ge(silu_ready, i + 1)
                dve.wait_ge(upped, i + 1)
                tt(h_e, banks[3][:, :], h_e, ALU.mult).then_inc(he_ready, 1)
                dve.wait_ge(put_turned, i + 1)
                copy(put.rearrange("p m t -> p (m t)"), banks[1][:, 0:S]).then_inc(put_ready, 1)
                if not last:
                    choose_gates(i + 1, pair + 1)
                    gather(i + 1)
                dve.wait_ge(downed, i + 1)
                copy(y_e[:, 512:1024], banks[3][:, :]).then_inc(ye_d, 1)

            choose(0, 0, True)
            choose_gates(0, 0)
            gather(0)
            with dve.Fori(0, PAIRS - 1) as i:
                experts(i, i)
            experts(PAIRS - 1, PAIRS - 1, True)
            with dve.If(fullest > SLOTS):
                for r in range(1, PASSES):
                    ts(place, place, -float(SLOTS), None, ALU.add).then_inc(moved, 1)
                    dve.wait_ge(moved, r)
                    choose(r * PAIRS, 0)
                    choose_gates(r * PAIRS, 0)
                    gather(r * PAIRS)
                    with dve.Fori(0, PAIRS - 1) as j:
                        experts(r * PAIRS + j, j)
                    experts(r * PAIRS + PAIRS - 1, PAIRS - 1, True)
            dve.wait_ge(y_summed, 1)
            for b in range(4):
                part = x[:, b // 2, 512 * (b % 2):512 * (b % 2) + 512]
                tt(part, banks[4 + b][:, :], part, ALU.add).then_inc(x_ready, 1)
            dve.wait_ge(x_ready, X_MOE)
            sum_squares(x, D, xn)
            rstd(MT, D)
            for m in range(MT):
                stt(xn[:, m, :], x[:, m, :], stats[:, 8 + m:9 + m], gains[:, 1, :], ALU.mult, ALU.mult).then_inc(out_ready, 1)


_INS = ['x', 'p', 'norm_mix_g', 'w_in', 'w_sgu_spatial', 'b_sgu_spatial', 'ln_v_g', 'ln_v_b', 'rel_bias', 'w_out',
        'norm_ffn_g', 'w_ff1', 'w_ff2', 'norm_ple_g', 'w_ple_gate', 'w_ple_proj', 'norm_final_g', 'norm_mix_2',
        'w_in_2', 'conv_w_2', 'conv_b_2', 'dt_bias_2', 'a_log_2', 'd_skip_2', 'ssd_norm_2', 'attn_sinks_2',
        'attn_norm_2', 'w_out_2', 'norm_ffn_2', 'w_router_group_2', 'w_router_expert_2', 'w_gate_2', 'w_up_2',
        'w_down_2', 'norm_final_2']


def bucket_line():
    distance = np.arange(LINE) - (P - 1)
    exact = BUCKETS // 2
    n = np.maximum(distance, exact)
    large = exact + np.floor(np.log(n / exact) / np.log(1024 / exact) * (BUCKETS - exact) + 1e-9).astype(int)
    bucket = np.where(distance < exact, distance, np.minimum(large, BUCKETS - 1))
    line = np.zeros((BUCKETS + 1, LINE), np.float32)
    line[np.maximum(bucket, 0), np.arange(LINE)] = distance >= 0
    line[BUCKETS, :P - 1] = MASKED
    return line


def kernel(**inputs):
    import concourse.bacc as _bacc
    from concourse.bass_utils import run_bass_kernel_spmd as _run

    nc = _bacc.Bacc("TRN2", target_bir_lowering=False, num_devices=1)
    arrays, args = {}, []
    given = [(name, np.ascontiguousarray(inputs[name])) for name in _INS] + [("bucket_line", bucket_line())]
    for name, a in given:
        arrays[f"in_{name}_dram"] = a
        args.append(nc.dram_tensor(f"in_{name}_dram", a.shape, mybir.dt.from_np(a.dtype), kind="ExternalInput").ap())
    out = nc.dram_tensor("out_0_dram", (1, S, D), F32, kind="ExternalOutput").ap()
    program(nc, *args, out)
    r = _run(nc, [arrays], core_ids=[0])
    return r.results[0]["out_0_dram"]
```
